# Optimizing a Trainium2 kernel written in Bass

```python
import jax, jax.numpy as jnp
from jax import lax
import numpy as np

D_MODEL = 2048
BATCH = 1
SEQ = 512
DEPTH = 1

GRID_W = 64
CTX_LEN = 256
D_MIX = D_MODEL
D_FOURIER = D_MIX // 2
N_FOURIER_GROUPS = 4
FOURIER_GROUP = D_FOURIER // N_FOURIER_GROUPS
D_LRU = D_MIX - D_FOURIER
N_LRU_HEADS = 8
LRU_HEAD = D_LRU // N_LRU_HEADS
LRU_CONV = 4
LRU_C = 8.0
D_FF = 5632
FFN_CONV = 3
N_MOD = 6
EPS = 1e-6
POS_BASE = 10000.0

kernel_name = "hybrid_fourier_rglru_dit_block"

def rms_norm(x, g):
    xf = x.astype(jnp.float32)
    y = xf * lax.rsqrt(jnp.mean(xf * xf, axis=-1, keepdims=True) + EPS)
    return (y * g.astype(jnp.float32)).astype(x.dtype)

def depthwise_conv(x, w, b, left):
    k_w = w.shape[0]
    n = x.shape[1]
    xp = jnp.pad(x, ((0, 0), (left, k_w - 1 - left), (0, 0)))
    y = b
    for k in range(k_w):
        y = y + xp[:, k:k + n] * w[k]
    return y

def grid_pos_embed(n_tokens, dtype):
    rows = n_tokens // GRID_W
    row = jnp.repeat(jnp.arange(rows, dtype=jnp.float32), GRID_W)
    col = jnp.tile(jnp.arange(GRID_W, dtype=jnp.float32), rows)
    quarter = D_MODEL // 4
    freqs = POS_BASE ** (-jnp.arange(quarter, dtype=jnp.float32) / quarter)

    def enc(p):
        ang = p[:, None] * freqs[None, :]
        return jnp.concatenate([jnp.sin(ang), jnp.cos(ang)], axis=-1)

    return jnp.concatenate([enc(row), enc(col)], axis=-1).astype(dtype)

def modulation(cond, w_ada, b_ada):
    m = jax.nn.silu(cond) @ w_ada + b_ada
    return [t[:, None, :] for t in jnp.split(m, N_MOD, axis=-1)]

def modulate(h, shift, scale):
    return h * (1 + scale) + shift

def mixer_inputs(h, w_in, conv_w, conv_b):
    proj = h @ w_in
    u_f, u_x, u_g = jnp.split(proj, [D_FOURIER, D_FOURIER + D_LRU], axis=-1)
    x_c = depthwise_conv(u_x, conv_w, conv_b, LRU_CONV // 2)
    return u_f, x_c, u_g

def lru_coeffs(x_c, w_a, b_a, w_x, b_x, lam):
    bsz, n, _ = x_c.shape
    xh = x_c.reshape(bsz, n, N_LRU_HEADS, LRU_HEAD)
    r = jax.nn.sigmoid((jnp.einsum('blhi,hij->blhj', xh, w_a).reshape(bsz, n, D_LRU) + b_a).astype(jnp.float32))
    i = jax.nn.sigmoid((jnp.einsum('blhi,hij->blhj', xh, w_x).reshape(bsz, n, D_LRU) + b_x).astype(jnp.float32))
    log_a = LRU_C * r * jax.nn.log_sigmoid(lam.astype(jnp.float32))
    a = jnp.exp(log_a)
    inp = jnp.sqrt(-jnp.expm1(2.0 * log_a)) * i * x_c.astype(jnp.float32)
    return a, inp

def linear_scan(a, b, h0, reverse):
    if h0 is not None:
        if reverse:
            b = b.at[:, -1].add(a[:, -1] * h0)
        else:
            b = b.at[:, 0].add(a[:, 0] * h0)

    def combine(e1, e2):
        a1, b1 = e1
        a2, b2 = e2
        return a1 * a2, a2 * b1 + b2

    _, h = lax.associative_scan(combine, (a, b), reverse=reverse, axis=1)
    return h

def bi_rglru(x_c, w_a, b_a, w_x, b_x, lam, h0_fwd, h0_bwd):
    a_f, i_f = lru_coeffs(x_c, w_a[0], b_a[0], w_x[0], b_x[0], lam[0])
    h_f = linear_scan(a_f, i_f, h0_fwd, reverse=False)
    a_b, i_b = lru_coeffs(x_c, w_a[1], b_a[1], w_x[1], b_x[1], lam[1])
    h_b = linear_scan(a_b, i_b, h0_bwd, reverse=True)
    return h_f, h_b

def fourier_mix(u_f, w_f, b_f):
    bsz, n, _ = u_f.shape
    ug = u_f.reshape(bsz, n, N_FOURIER_GROUPS, FOURIER_GROUP).astype(jnp.float32)
    f = jnp.fft.fft2(ug, axes=(1, 3), norm="ortho").real.astype(u_f.dtype)
    y = jnp.einsum('blgc,gcd->blgd', f, w_f).reshape(bsz, n, D_FOURIER)
    return y + b_f

def mixer_output(u_f, h_f, h_b, u_g, w_f, b_f, w_out):
    y_fourier = fourier_mix(u_f, w_f, b_f)
    y_lru = (h_f + h_b).astype(u_g.dtype) * jax.nn.gelu(u_g, approximate=True)
    return jnp.concatenate([y_fourier, y_lru], axis=-1) @ w_out

def conv_ffn(h, w_up, conv_w, conv_b, w_down):
    up = depthwise_conv(h @ w_up, conv_w, conv_b, FFN_CONV // 2)
    g, v = jnp.split(up, 2, axis=-1)
    return (jax.nn.gelu(g, approximate=True) * v) @ w_down

def setup_inputs(seed: int = 0) -> dict:
    key = jax.random.key(seed)
    ks = jax.random.split(key, 32)
    f32 = jnp.float32
    nrm = lambda k, shape, s: jax.random.normal(k, shape, f32) * s
    u = jax.random.uniform(ks[16], (DEPTH, 2, D_LRU), f32, 0.9, 0.999)
    a_base = u ** (1.0 / LRU_C)
    lam = jnp.log(a_base) - jnp.log1p(-a_base)
    return {
        "x": nrm(ks[0], (BATCH, SEQ, D_MODEL), 1.0),
        "c": nrm(ks[1], (BATCH, D_MODEL), 1.0),
        "ctx": nrm(ks[2], (BATCH, CTX_LEN, D_MODEL), 1.0),
        "c_ctx": nrm(ks[3], (D_MODEL,), 1.0),
        "w_ada": nrm(ks[4], (DEPTH, D_MODEL, N_MOD * D_MODEL), 0.5 * D_MODEL ** -0.5),
        "b_ada": nrm(ks[5], (DEPTH, N_MOD * D_MODEL), 0.01),
        "g_mix_pre": 1.0 + nrm(ks[6], (DEPTH, D_MODEL), 0.02),
        "g_mix_post": 1.0 + nrm(ks[7], (DEPTH, D_MODEL), 0.02),
        "g_ffn_pre": 1.0 + nrm(ks[8], (DEPTH, D_MODEL), 0.02),
        "g_ffn_post": 1.0 + nrm(ks[9], (DEPTH, D_MODEL), 0.02),
        "w_in": nrm(ks[10], (DEPTH, D_MODEL, D_FOURIER + 2 * D_LRU), D_MODEL ** -0.5),
        "conv_lru_w": nrm(ks[11], (DEPTH, LRU_CONV, D_LRU), LRU_CONV ** -0.5),
        "conv_lru_b": nrm(ks[12], (DEPTH, D_LRU), 0.01),
        "w_rec_gate": nrm(ks[13], (DEPTH, 2, N_LRU_HEADS, LRU_HEAD, LRU_HEAD), LRU_HEAD ** -0.5),
        "b_rec_gate": nrm(ks[14], (DEPTH, 2, D_LRU), 0.01),
        "w_in_gate": nrm(ks[15], (DEPTH, 2, N_LRU_HEADS, LRU_HEAD, LRU_HEAD), LRU_HEAD ** -0.5),
        "b_in_gate": nrm(ks[17], (DEPTH, 2, D_LRU), 0.01),
        "lru_lambda": lam,
        "w_fourier": nrm(ks[18], (DEPTH, N_FOURIER_GROUPS, FOURIER_GROUP, FOURIER_GROUP), FOURIER_GROUP ** -0.5),
        "b_fourier": nrm(ks[19], (DEPTH, D_FOURIER), 0.01),
        "w_out": nrm(ks[20], (DEPTH, D_MIX, D_MODEL), D_MIX ** -0.5),
        "w_up": nrm(ks[21], (DEPTH, D_MODEL, 2 * D_FF), D_MODEL ** -0.5),
        "conv_ffn_w": nrm(ks[22], (DEPTH, FFN_CONV, 2 * D_FF), FFN_CONV ** -0.5),
        "conv_ffn_b": nrm(ks[23], (DEPTH, 2 * D_FF), 0.01),
        "w_down": nrm(ks[24], (DEPTH, D_FF, D_MODEL), D_FF ** -0.5),
    }

def reference(x, c, ctx, c_ctx, w_ada, b_ada, g_mix_pre, g_mix_post, g_ffn_pre, g_ffn_post,
              w_in, conv_lru_w, conv_lru_b, w_rec_gate, b_rec_gate, w_in_gate, b_in_gate,
              lru_lambda, w_fourier, b_fourier, w_out, w_up, conv_ffn_w, conv_ffn_b, w_down):
    n_lat = x.shape[1]
    x = x + grid_pos_embed(n_lat, x.dtype)[None]
    for l in range(DEPTH):
        last = l == DEPTH - 1
        sh1, sc1, gt1, sh2, sc2, gt2 = modulation(c, w_ada[l], b_ada[l])
        csh1, csc1, cgt1, csh2, csc2, cgt2 = modulation(c_ctx[None], w_ada[l], b_ada[l])
        lru_p = (w_rec_gate[l], b_rec_gate[l], w_in_gate[l], b_in_gate[l], lru_lambda[l])

        hc = modulate(rms_norm(ctx, g_mix_pre[l]), csh1, csc1)
        uf_c, xc_c, ug_c = mixer_inputs(hc, w_in[l], conv_lru_w[l], conv_lru_b[l])
        hf_c, hb_c = bi_rglru(xc_c, *lru_p, None, None)

        hx = modulate(rms_norm(x, g_mix_pre[l]), sh1, sc1)
        uf_x, xc_x, ug_x = mixer_inputs(hx, w_in[l], conv_lru_w[l], conv_lru_b[l])
        hf_x, hb_x = bi_rglru(xc_x, *lru_p, hf_c[:, -1], hb_c[:, 0])
        y_x = mixer_output(uf_x, hf_x, hb_x, ug_x, w_fourier[l], b_fourier[l], w_out[l])
        x = x + gt1 * rms_norm(y_x, g_mix_post[l])

        hx2 = modulate(rms_norm(x, g_ffn_pre[l]), sh2, sc2)
        x = x + gt2 * rms_norm(conv_ffn(hx2, w_up[l], conv_ffn_w[l], conv_ffn_b[l], w_down[l]), g_ffn_post[l])

        if not last:
            y_c = mixer_output(uf_c, hf_c, hb_c, ug_c, w_fourier[l], b_fourier[l], w_out[l])
            ctx = ctx + cgt1 * rms_norm(y_c, g_mix_post[l])
            hc2 = modulate(rms_norm(ctx, g_ffn_pre[l]), csh2, csc2)
            ctx = ctx + cgt2 * rms_norm(conv_ffn(hc2, w_up[l], conv_ffn_w[l], conv_ffn_b[l], w_down[l]), g_ffn_post[l])
    return x


_drawn_inputs = setup_inputs


def setup_inputs(seed=0):
    import zlib

    import numpy as np

    out = dict(_drawn_inputs(seed))
    spreads = {}
    factors = {'ctx': 5.817,
     'b_ada': 4.136,
     'g_mix_pre': 7.998,
     'g_mix_post': 8.0,
     'g_ffn_pre': 24.392,
     'g_ffn_post': 31.977,
     'conv_lru_b': 8.0,
     'b_rec_gate': 64.0,
     'b_in_gate': 64.0,
     'b_fourier': 64.0,
     'conv_ffn_b': 49.079}
    for name, (base, spread) in spreads.items():
        noise = np.random.default_rng([zlib.crc32(name.encode()), seed]).standard_normal(out[name].shape)
        drawn = base * np.exp(spread * noise) if base else spread * noise
        out[name] = __import__('jax').numpy.asarray(drawn.astype(out[name].dtype))
    for name, factor in factors.items():
        out[name] = (out[name] * factor).astype(out[name].dtype)
    return out
```

```python
from contextlib import ExitStack, contextmanager

import numpy as np

import concourse.bass as bass
from concourse import mybir

F32 = mybir.dt.float32
F32R = mybir.dt.float32r
ALU = mybir.AluOpType
ACT = mybir.ActivationFunctionType
ds = bass.ds

P = 128
D = 2048
KT = D // P
L = 512
C = 256
GRID = 64
HEADS = 8
GROUPS = 4
GW = 256
FT = 5632 // P
CH = 4
NCH = FT // CH
RING = 4
UNIT = 8 * P
NFREQ = L // 2 + 2
EPS = 1e-6

U_HEADS = 4 * HEADS
U_FOUR = 4 * GROUPS
U_OUT = 2 * KT
U_FFN = 2 * 2 * FT + NCH * KT // 2
UNITS = U_HEADS + U_FOUR + U_OUT + U_FFN
NADA = 4
ASLOTS = 4
ACOL = 256
NBG = (6 * D - NADA * 1024) // ACOL
BGU = KT // 2
LAST_ADA = NBG - 1

PAR = {}
NPAR = 0
for _name, _n in (("ones", P), ("ident", P), ("cond", 2 * KT), ("b_ada", 6 * KT), ("g_mix_pre", KT), ("g_mix_post", KT),
                  ("g_ffn_pre", KT), ("g_ffn_post", KT), ("lam", 2 * HEADS), ("b_fourier", 8), ("lru_conv_w", 4 * HEADS),
                  ("lru_conv_b", HEADS), ("gate_b", 4 * HEADS)):
    PAR[_name] = (NPAR, _n)
    NPAR += _n
LATE = {}
NPOS = NLATE = 0
for _name, _n in (("row_pos", 8 * (L // GRID)), ("col_pos", 8 * GRID), ("ffn_conv_w", 3 * 2 * FT), ("ffn_conv_b", 2 * FT)):
    LATE[_name] = (NLATE, _n)
    NLATE += _n
    if _name == "col_pos":
        NPOS = NLATE


class Chain:

    def __init__(self, eng, sem):
        self.eng, self.sem, self.base, self.k = eng, sem, 0, 0

    def step(self, ins):
        ins.then_inc(self.sem, 1)
        self.k += 1

    def wait(self):
        self.eng.wait_ge(self.sem, self.base + self.k)

    @contextmanager
    def loop(self, start, stop, per):
        first = self.base + self.k
        with self.eng.Fori(start, stop) as i:
            self.base, self.k = (i - start) * per + first, 0
            yield i
            assert self.k == per, (self.k, per)
        self.base, self.k = first + (stop - start) * per, 0


def build(nc, x_t, ctx_t, par_d, late_d, stream, ada0, adabg, gates_d, tabs_d, out_t):
    ctx = ExitStack()
    with ctx:
        def sem(name):
            return ctx.enter_context(nc.semaphore(name))

        def sbuf(stack, name, shape, dt=F32, side=None):
            return stack.enter_context(nc.sbuf_tensor(name, shape, dt, side=side))

        par = sbuf(ctx, "par", [P, NPAR])
        h_hi = sbuf(ctx, "h_hi", [P, KT, L], F32R)
        h_lo = sbuf(ctx, "h_lo", [P, KT, L], F32R)
        w_raw = sbuf(ctx, "w_raw", [P, RING, UNIT])
        w_hi = sbuf(ctx, "w_hi", [P, RING, UNIT], F32R)
        w_lo = sbuf(ctx, "w_lo", [P, RING, UNIT], F32R)
        csil = sbuf(ctx, "csil", [P, 2 * KT])
        mod_x = sbuf(ctx, "mod_x", [P, 6 * KT])
        mod_c = sbuf(ctx, "mod_c", [P, 2 * KT])
        gain = sbuf(ctx, "gain", [P, 5 * KT])
        small = sbuf(ctx, "small", [P, 9 * KT])
        decay = sbuf(ctx, "decay", [P, 3, 2 * HEADS])

        def pcol(name, a=0, n=None):
            at, width = PAR[name]
            return par[:, ds(at + a, width if n is None else n)]

        def lcol(t, name, a=0, n=None):
            at, width = LATE[name]
            return t[:, ds(at + a, width if n is None else n)]

        def tile(t, k, a=0, b=L):
            return t[:, ds(k * L + a, b - a)]

        ones, ident = pcol("ones"), pcol("ident")
        gain_x, gain_c, gain_y, gain_f, gain_d = (gain[:, KT * i:KT * i + KT] for i in range(5))

        with ExitStack() as s:
            hc_hi = sbuf(s, "hc_hi", [P, KT, C], F32R)
            hc_lo = sbuf(s, "hc_lo", [P, KT, C], F32R)
            x0 = sbuf(s, "x0", [P, KT, L])
            c0 = sbuf(s, "c0", [P, KT, C])
            sq0 = sbuf(s, "sq0", [P, 2, L])
            ss_x = sbuf(s, "ss_x", [P, L])
            ss_c = sbuf(s, "ss_c", [P, C])
            pos0 = sbuf(s, "pos0", [P, NPOS])

        mix = ExitStack()
        ada_raw = sbuf(mix, "ada_raw", [P, ASLOTS, 2 * ACOL], side="right")
        ada_acc = sbuf(mix, "ada_acc", [P, ACOL], side="right")
        with ExitStack() as late:
            y_lru = sbuf(late, "y_lru", [P, HEADS * L], side="right")
            with ExitStack() as s:
                sbuf(s, "hc_hi_kept", [P, KT, C])
                sbuf(s, "hc_lo_kept", [P, KT, C])
                xc = sbuf(s, "xc", [P, C + L])
                xc_hi = sbuf(s, "xc_hi", [P, C + L], F32R)
                xc_lo = sbuf(s, "xc_lo", [P, C + L], F32R)
                lru_r = sbuf(s, "lru_r", [P, 2, C + L])
                lru_i = sbuf(s, "lru_i", [P, 2, C + L])
                lru_u = sbuf(s, "lru_u", [P, 2, C + L])
                g_raw = sbuf(s, "g_raw", [P, 4 * P])
                g_hi = sbuf(s, "g_hi", [P, 4 * P], F32R)
                g_lo = sbuf(s, "g_lo", [P, 4 * P], F32R)
            with ExitStack() as s:
                y_four = sbuf(s, "y_four", [P, 8 * L])
                u_sb = sbuf(s, "u_sb", [P, L])
                eo = sbuf(s, "eo", [P, 2, C])
                eo_hi = sbuf(s, "eo_hi", [P, 2, 2, C], F32R)
                eo_lo = sbuf(s, "eo_lo", [P, 2, 2, C], F32R)
                nyq = sbuf(s, "nyq", [P, 2, 2], F32R)
                nyq_p = sbuf(s, "nyq_p", [P, 10])
                tab_raw = sbuf(s, "tab_raw", [P, 2 * NFREQ])
                tok_hi = sbuf(s, "tok_hi", [P, 2, 2 * NFREQ], F32R)
                tok_lo = sbuf(s, "tok_lo", [P, 2, 2 * NFREQ], F32R)
                chan_hi = sbuf(s, "chan_hi", [P, 2, 2 * GW], F32R)
                chan_lo = sbuf(s, "chan_lo", [P, 2, 2 * GW], F32R)
                wf_hi = sbuf(s, "wf_hi", [P, 2, GW], F32R)
                wf_lo = sbuf(s, "wf_lo", [P, 2, GW], F32R)
                m_hi = sbuf(s, "m_hi", [P, 2, 2 * GW], F32R)
                m_lo = sbuf(s, "m_lo", [P, 2, 2 * GW], F32R)
                p_hi = sbuf(s, "p_hi", [P, 2, 2 * GW], F32R)
                p_lo = sbuf(s, "p_lo", [P, 2, 2 * GW], F32R)
        fin = ExitStack()
        x1 = sbuf(fin, "x1", [P, KT, L])
        acc = sbuf(fin, "acc", [P, KT * L])
        late_par = sbuf(fin, "late_par", [P, NLATE])
        with ExitStack() as s:
            sq1 = sbuf(s, "sq1", [P, 2, L])
            ss1 = sbuf(s, "ss1", [P, L])
        mix.close()
        with ExitStack() as s:
            cg = sbuf(s, "cg", [P, 2, L])
            cv = sbuf(s, "cv", [P, L])
            ss2 = sbuf(s, "ss2", [P, L])
            act_hi = sbuf(s, "act_hi", [P, CH, L], F32R)
            act_lo = sbuf(s, "act_lo", [P, CH, L], F32R)
        fin.close()

        bank = [ctx.enter_context(nc.psum_tensor(f"bank{i}", [P, 512], F32)) for i in range(8)]

        par_in, pos_in, late_in = sem("par_in"), sem("pos_in"), sem("late_in")
        x_in, c_in = [sem(f"x_in{i}") for i in range(4)], sem("c_in")
        raw_in = [sem(f"raw_in{i}") for i in range(RING)]
        hi_done, lo_done = sem("hi_done"), sem("lo_done")
        ada0_used = sem("ada0_used")
        ada_in = [sem(f"ada_in{i}") for i in range(ASLOTS)]
        rows_copied, turned, mod_made = sem("rows_copied"), sem("turned"), sem("mod_made")
        ada_eaten, ada_summed, ada_read = sem("ada_eaten"), sem("ada_summed"), sem("ada_read")
        act_chain, dve_chain = sem("act_chain"), sem("dve_chain")
        csig_done, csil_done, exp_lam, decay_done = sem("csig_done"), sem("csil_done"), sem("exp_lam"), sem("decay_done")
        x_posed, sq_done, sq_added = sem("x_posed"), sem("sq_done"), sem("sq_added")
        totals, var_done, std_done, rms_done = (sem(n) for n in ("totals", "var_done", "std_done", "rms_done"))
        h_pre, h_rounded, h_ready = sem("h_pre"), sem("h_rounded"), sem("h_ready")
        ux_done, ug_done, gates_done = sem("ux_done"), sem("ug_done"), sem("gates_done")
        xc_seed, xc_done, xc_round, xc_split = sem("xc_seed"), sem("xc_done"), sem("xc_round"), sem("xc_split")
        gate_in, gate_hi, gate_lo = sem("gate_in"), sem("gate_hi"), sem("gate_lo")
        gelu_done, gates_read, exp_done, gap_done, root_done, scan_done, head_done = (
            sem(n) for n in ("gelu_done", "gates_read", "exp_done", "gap_done", "root_done", "scan_done", "head_done"))
        tab_in, tab_hi, tab_lo = sem("tab_in"), sem("tab_hi"), sem("tab_lo")
        uf_done, uf_copied, eo_done, eo_rounded, eo_split = (
            sem(n) for n in ("uf_done", "uf_copied", "eo_done", "eo_rounded", "eo_split"))
        m_done, m_rounded, m_split = sem("m_done"), sem("m_rounded"), sem("m_split")
        nyq_done, nyq_read = sem("nyq_done"), sem("nyq_read")
        p_done, p_rounded, p_split = sem("p_done"), sem("p_rounded"), sem("p_split")
        yf_done, yf_read = sem("yf_done"), sem("yf_read")
        yc_rounded, yc_ready = sem("yc_rounded"), sem("yc_ready")
        y_done, y_copied = sem("y_done"), sem("y_copied")
        y_normed, x1_done, x1_squared, x1_summed = (
            sem("y_normed"), (sem("x1_dve"), sem("x1_pool")), sem("x1_squared"), sem("x1_summed"))
        h2_pre, h2_rounded, h2_ready = ((sem(n + "_dve"), sem(n + "_pool")) for n in ("h2_pre", "h2_rounded", "h2_ready"))
        up_g, up_v, seed_g, seed_v = sem("up_g"), sem("up_v"), sem("seed_g"), sem("seed_v")
        conv_g, conv_v, ffn_gelu, ffn_prod = sem("conv_g"), sem("conv_v"), sem("ffn_gelu"), sem("ffn_prod")
        ffn_round, ffn_split = sem("ffn_round"), sem("ffn_split")
        down_done, down_added = sem("down_done"), sem("down_added")
        f_normed, out_ready, stored = sem("f_normed"), (sem("out_dve"), sem("out_pool")), sem("stored")

        block = ctx.enter_context(nc.Block())

        GATE_BANKS = ((3, 5), (6, 1))
        POOL_SUM = [k for k in range(KT) if k % 3 != 2]
        POOL_H2 = [k for k in range(KT) if k % 3 == 2]

        def shared(sems, pool_tiles, k):
            mine = k in pool_tiles
            return sems[mine], sum((j in pool_tiles) == mine for j in range(k + 1))

        R_FOUR = U_HEADS // RING
        R_OUT = R_FOUR + U_FOUR // RING
        R_FFN = R_OUT + U_OUT // RING
        ROUNDS = UNITS // RING
        ADA_ROUNDS = NADA * KT // RING

        @block.sync
        def _(sp):
            def load_unit(rnd, s):
                if isinstance(rnd, int) and rnd == 0:
                    sp.wait_ge(ada0_used, NADA * KT - RING + s + 1)
                else:
                    sp.wait_ge(lo_done, rnd * RING + s - 3)
                sp.dma_start(w_raw[:, s, :], stream[rnd * RING + s]).then_inc(raw_in[s], 16)

            def load_ada(chunk, q):
                if not (isinstance(chunk, int) and chunk == 0 and q < ASLOTS):
                    sp.wait_ge(ada_eaten, chunk * BGU + q - ASLOTS + 1)
                sp.dma_start(ada_raw[:, q % ASLOTS, :], adabg[chunk * BGU + q]).then_inc(ada_in[q % ASLOTS], 16)

            def load_ada0(r):
                for s in range(RING):
                    if not isinstance(r, int) or r > 0:
                        sp.wait_ge(ada0_used, r * RING + s - 3)
                    sp.dma_start(w_raw[:, s, :], ada0[r * RING + s]).then_inc(raw_in[s], 16)

            sp.dma_start(par[:, :], par_d).then_inc(par_in, 16)
            load_ada0(0)
            sp.dma_start(pos0[:, :], late_d[:, 0:NPOS]).then_inc(pos_in, 16)
            for i in range(4):
                sp.dma_start(x0[:, 4 * i:4 * i + 4, :], x_t[:, 4 * i:4 * i + 4, :]).then_inc(x_in[i], 16)
                load_ada0(i + 1)
            sp.dma_start(c0[:, :, :], ctx_t).then_inc(c_in, 16)
            with sp.Fori(5, ADA_ROUNDS) as r:
                load_ada0(r)
            for s in range(RING):
                load_unit(0, s)

            def head_loads(h):
                if not isinstance(h, int):
                    sp.wait_ge(gate_lo, h)
                sp.dma_start(g_raw[:, :], gates_d[h]).then_inc(gate_in, 16)
                if isinstance(h, int):
                    for q in range(BGU):
                        load_ada(0, q)
                for s in range(RING):
                    load_unit(h + 1, s)
                    load_ada(h + 1, 2 * s)
                    load_ada(h + 1, 2 * s + 1)

            sp.wait_ge(h_ready, KT)
            head_loads(0)
            with sp.Fori(1, HEADS) as h:
                head_loads(h)

            for s in range(RING):
                load_unit(R_FOUR + 1, s)
            sp.wait_ge(head_done, HEADS)
            for n in range(4):
                sp.dma_start(y_four[:, ds(n * 2 * NFREQ, 2 * NFREQ)], tabs_d[n]).then_inc(tab_in, 16)

            def four_loads(g):
                if not isinstance(g, int):
                    sp.wait_ge(tab_lo, g + 4)
                sp.dma_start(tab_raw[:, :], tabs_d[g + 4]).then_inc(tab_in, 16)
                for s in range(RING):
                    load_unit(g + R_FOUR + 2, s)
                    for q in range(4):
                        load_ada(g * 2 + HEADS + 1 + s // 2, 4 * (s % 2) + q)

            four_loads(0)
            with sp.Fori(1, GROUPS) as g:
                four_loads(g)

            sp.wait_ge(yc_ready, KT)
            for i in range(4):
                sp.dma_start(x1[:, 4 * i:4 * i + 4, :], x_t[:, 4 * i:4 * i + 4, :]).then_inc(x_in[i], 16)
            sp.dma_start(late_par[:, :], late_d).then_inc(late_in, 16)

            def out_loads(i, chunks):
                for s in range(RING):
                    load_unit(i + R_OUT + 2, s)
                    for q in range(2 * chunks):
                        load_ada(i * 2 + HEADS + 2 * GROUPS + 1 + s * chunks // 4, 2 * chunks * s % BGU + q)

            with sp.Fori(0, KT // 2 - 1) as i:
                out_loads(i, 2)
            out_loads(KT // 2 - 1, 1)
            with sp.Fori(R_FFN + 2, ROUNDS) as r:
                for s in range(RING):
                    load_unit(r, s)

            for k in range(KT):
                sp.wait_ge(*shared(out_ready, POOL_SUM, k))
                sp.dma_start(out_t[:, k, :], x1[:, k, :]).then_inc(stored, 16)
            sp.wait_ge(stored, 16 * KT)

        @block.gpsimd
        def _(pool):
            def remainders(r):
                for s in range(RING):
                    pool.wait_ge(hi_done, r * RING + s + 1)
                    nc.gpsimd.tensor_tensor(w_lo[:, s, :], w_raw[:, s, :], w_hi[:, s, :].bitcast(F32),
                                            ALU.subtract).then_inc(lo_done, 1)

            with pool.Fori(0, R_FFN + 1) as r:
                remainders(r)
            for n, k in enumerate(POOL_SUM):
                pool.wait_ge(y_normed, n + 1)
                nc.gpsimd.tensor_tensor(x1[:, k, :], x1[:, k, :], tile(acc, k), ALU.add).then_inc(x1_done[1], 1)
            pool.wait_ge(rms_done, 4)
            for n in range(len(POOL_H2) + 1):
                if n < len(POOL_H2):
                    k = POOL_H2[n]
                    nc.gpsimd.tensor_tensor(tile(acc, k), x1[:, k, :], ss1[:, :], ALU.mult).then_inc(h2_pre[1], 1)
                if n > 0:
                    k = POOL_H2[n - 1]
                    pool.wait_ge(h2_rounded[1], n)
                    nc.gpsimd.tensor_tensor(h_lo[:, k, :], tile(acc, k), h_hi[:, k, :].bitcast(F32),
                                            ALU.subtract).then_inc(h2_ready[1], 1)
            with pool.Fori(R_FFN + 1, ROUNDS) as r:
                remainders(r)
            for n, k in enumerate(POOL_SUM):
                pool.wait_ge(f_normed, n + 1)
                nc.gpsimd.tensor_tensor(x1[:, k, :], x1[:, k, :], tile(acc, k), ALU.add).then_inc(out_ready[1], 1)

        @block.scalar
        def _(act):
            chain = Chain(act, act_chain)
            sq_n = [0]

            def round_unit(rnd, s):
                act.wait_ge(raw_in[s], rnd * 16 + 16 * (ADA_ROUNDS + 1))
                nc.scalar.activation(w_hi[:, s, :], w_raw[:, s, :], ACT.Copy).then_inc(hi_done, 1)

            def square(dst, src, n):
                if not (isinstance(n, int) and n < 2):
                    act.wait_ge(sq_added, n - 1)
                nc.scalar.activation(dst, src, ACT.Square).then_inc(sq_done, 1)

            def std(n, rms):
                act.wait_ge(var_done, n + 1)
                nc.scalar.activation(rms, rms, ACT.Sqrt).then_inc(std_done, 1)

            act.wait_ge(par_in, 16)
            nc.scalar.activation(csil[:, :], pcol("cond"), ACT.Sigmoid).then_inc(csig_done, 1)
            chain.step(nc.scalar.activation(decay[:, 0, :], pcol("lam"), ACT.Abs))
            chain.wait()
            nc.scalar.activation(decay[:, 1, :], decay[:, 0, :], ACT.Exp, scale=-1.0).then_inc(exp_lam, 1)
            for k in range(KT):
                act.wait_ge(x_posed, k // 4 + 1)
                square(sq0[:, k % 2, :], x0[:, k, :], k)
            act.wait_ge(c_in, 16)
            for k in range(KT):
                square(sq0[:, k % 2, 0:C], c0[:, k, :], KT + k)
            std(0, ss_x[:, :])
            std(1, ss_c[:, :])
            for c in range(NADA):
                for half in range(2):
                    act.wait_ge(ada0_used, 16 * c + 8 * half + 8)
                    if c > 0:
                        act.wait_ge(turned, c)
                    elif half == 0:
                        act.wait_ge(sq_added, 2 * KT)
                    nc.scalar.activation(sq0[0:2, half, :], bank[half][0:2, :], ACT.Copy).then_inc(rows_copied, 1)
                if c == NADA - 1:
                    round_unit(0, 0)
                    round_unit(0, 1)
                for k in range(4 * c, 4 * c + 4):
                    act.wait_ge(h_pre, 2 * k + 1)
                    nc.scalar.activation(h_hi[:, k, :], x0[:, k, :], ACT.Identity,
                                         bias=mod_x[:, k:k + 1]).then_inc(h_rounded, 1)
                    act.wait_ge(h_pre, 2 * k + 2)
                    nc.scalar.activation(hc_hi[:, k, :], c0[:, k, :], ACT.Identity,
                                         bias=mod_c[:, k:k + 1]).then_inc(h_rounded, 1)
            round_unit(0, 2)
            round_unit(0, 3)
            act.wait_ge(decay_done, 1)

            def head(h):
                first = isinstance(h, int)
                act.wait_ge(gate_in, h * 16 + 16)
                if not first:
                    act.wait_ge(gates_done, h * 2)
                nc.scalar.activation(g_hi[:, :], g_raw[:, :], ACT.Copy).then_inc(gate_hi, 1)
                act.wait_ge(ux_done, h + 1)
                taps = pcol("lru_conv_w", h * 4 + 2, 1)
                bias = pcol("lru_conv_b", h, 1)
                nc.scalar.activation(xc[:, C:C + L], bank[0][:, :], ACT.Identity, bias=bias, scale=taps).then_inc(xc_seed, 1)
                nc.scalar.activation(xc[:, 0:C], bank[2][:, 0:C], ACT.Identity, bias=bias, scale=taps).then_inc(xc_seed, 1)
                round_unit(h + 1, 0)
                round_unit(h + 1, 1)
                act.wait_ge(xc_done, h + 1)
                nc.scalar.activation(xc_hi[:, :], xc[:, :], ACT.Copy).then_inc(xc_round, 1)
                act.wait_ge(ug_done, h + 1)
                nc.scalar.activation(tile(y_lru, h), bank[1][:, :],
                                     ACT.Gelu_apprx_tanh).then_inc(gelu_done, 1)
                for d in range(2):
                    act.wait_ge(gates_done, h * 2 + d + 1)
                    if not first:
                        act.wait_ge(scan_done, h * 2 + d - 1)
                    br, bi = pcol("gate_b", h * 4 + 2 * d, 1), pcol("gate_b", h * 4 + 2 * d + 1, 1)
                    xb, cb = GATE_BANKS[d]
                    nc.scalar.activation(lru_r[:, d, C:C + L], bank[xb][:, :], ACT.Sigmoid, bias=br)
                    nc.scalar.activation(lru_i[:, d, C:C + L], bank[xb + 1][:, :], ACT.Sigmoid, bias=bi)
                    chain.step(nc.scalar.activation(lru_r[:, d, 0:C], bank[cb][:, 0:C], ACT.Sigmoid, bias=br))
                    nc.scalar.activation(lru_i[:, d, 0:C], bank[cb][:, C:2 * C], ACT.Sigmoid, bias=bi).then_inc(gates_read, 1)
                chain.wait()
                if not first:
                    act.wait_ge(head_done, h)
                for d in range(2):
                    chain.step(nc.scalar.activation(lru_u[:, d, :], lru_r[:, d, :], ACT.Tanh,
                                                    scale=decay[:, 1, ds(h * 2 + d, 1)]))
                for d in range(2):
                    nc.scalar.activation(lru_r[:, d, :], lru_r[:, d, :], ACT.Exp,
                                         scale=decay[:, 2, ds(h * 2 + d, 1)]).then_inc(exp_done, 1)
                round_unit(h + 1, 2)
                round_unit(h + 1, 3)
                for d in range(2):
                    act.wait_ge(gap_done, h * 2 + d + 1)
                    nc.scalar.activation(lru_u[:, d, :], lru_u[:, d, :], ACT.Sqrt).then_inc(root_done, 1)

            head(0)
            with chain.loop(1, HEADS, 4) as h:
                head(h)

            def round_table(n, dst, src):
                act.wait_ge(tab_in, 80 if isinstance(n, int) else n * 16 + 16)
                nc.scalar.activation(dst, src[:, 0:dst.shape[-1]], ACT.Copy).then_inc(tab_hi, 1)

            def fourier_input(g, t):
                n = g * 2 + t
                act.wait_ge(uf_done, n + 1)
                round_unit(g + R_FOUR + 1, 2 * t)
                round_unit(g + R_FOUR + 1, 2 * t + 1)
                if isinstance(g, int) and t == 0:
                    act.wait_ge(head_done, HEADS)
                else:
                    act.wait_ge(eo_split, n)
                nc.scalar.activation(u_sb[:, :], bank[t][:, :], ACT.Copy).then_inc(uf_copied, 1)
                act.wait_ge(eo_done, n + 1)
                if not (isinstance(g, int) and g == 0):
                    act.wait_ge(p_done, g)
                nc.scalar.activation(nyq[:, t, 0:1], u_sb[:, C:C + 1], ACT.Copy)
                nc.scalar.activation(eo_hi[:, t, :, :], eo[:, :, :], ACT.Copy).then_inc(eo_rounded, 1)

            def round_m(g):
                act.wait_ge(m_done, g + 1)
                for t in range(2):
                    nc.scalar.activation(m_hi[:, t, :], bank[6 + t][:, :], ACT.Copy).then_inc(m_rounded, 1)

            def round_p(g):
                act.wait_ge(p_done, g + 1)
                for t in range(2):
                    nc.scalar.activation(p_hi[:, t, :], bank[4 + t][:, :], ACT.Copy).then_inc(p_rounded, 1)

            def round_ycat(n, src):
                nc.scalar.activation(h_hi[:, n, :], src, ACT.Copy).then_inc(yc_rounded, 1)

            fourier_input(0, 0)
            for n in range(4):
                round_table(n, (chan_hi if n < 2 else tok_hi)[:, n % 2, :], y_four[:, ds(n * 2 * NFREQ, 2 * NFREQ)])
            wf_all = wf_hi[:, :, :].rearrange("p t d -> p (t d)")
            round_table(4, wf_all, tab_raw)
            fourier_input(0, 1)
            round_m(0)
            with act.Fori(1, GROUPS) as g:
                act.wait_ge(m_done, g)
                round_table(g + 4, wf_all, tab_raw)
                fourier_input(g, 0)
                round_p(g - 1)
                round_m(g)
                fourier_input(g, 1)
            for n in range(HEADS):
                round_ycat(n, tile(y_lru, n))
                if n == 3:
                    round_p(GROUPS - 1)
            for n in range(8):
                act.wait_ge(yf_read, n // 2 + 1)
                round_ycat(HEADS + n, tile(y_four, n))

            with act.Fori(0, KT // 2) as i:
                for t in range(2):
                    m = i * 2 + t
                    act.wait_ge(y_done, m + 1)
                    round_unit(i + R_OUT + 1, 2 * t)
                    round_unit(i + R_OUT + 1, 2 * t + 1)
                    nc.scalar.activation(tile(acc, m), bank[t][:, :], ACT.Copy).then_inc(y_copied, 1)
                    square(sq1[:, t, :], bank[t][:, :], m + 2 * KT)
            std(2, ss1[:, :])
            act.wait_ge(sq_added, 3 * KT)
            for k in range(KT):
                act.wait_ge(*shared(x1_done, POOL_SUM, k))
                if k > 1:
                    act.wait_ge(x1_summed, k - 1)
                nc.scalar.activation(sq1[:, k % 2, :], x1[:, k, :], ACT.Square).then_inc(x1_squared, 1)
            std(3, ss1[:, :])
            act.wait_ge(late_in, 16)
            for k in range(KT):
                shift = mod_x[:, 3 * KT + k:3 * KT + k + 1]
                act.wait_ge(*shared(h2_pre, POOL_H2, k))
                if k in POOL_H2:
                    chain.step(nc.scalar.activation(tile(acc, k), tile(acc, k), ACT.Identity,
                                                    bias=shift, scale=gain_f[:, k:k + 1]))
                    chain.wait()
                    nc.scalar.activation(h_hi[:, k, :], tile(acc, k), ACT.Copy).then_inc(h2_rounded[1], 1)
                else:
                    nc.scalar.activation(h_hi[:, k, :], tile(acc, k), ACT.Identity, bias=shift).then_inc(h2_rounded[0], 1)

            def seed(f, src, dst, tile, done):
                nc.scalar.activation(dst, src, ACT.Identity, bias=lcol(late_par, "ffn_conv_b", tile, 1),
                                     scale=lcol(late_par, "ffn_conv_w", tile * 3 + 1, 1)).then_inc(done, 1)

            def round_act(q):
                nc.scalar.activation(act_hi[:, q, :], cg[:, q % 2, :], ACT.Copy).then_inc(ffn_round, 1)

            def pair(c, p, rnd):
                n = c * CH + p
                act.wait_ge(up_g, n + 1)
                round_unit(rnd, 0)
                round_unit(rnd, 1)
                if not (isinstance(c, int) and p == 0):
                    act.wait_ge(ffn_prod, n)
                    if p > 0 and not isinstance(c, int):
                        act.wait_ge(down_done, c * KT)
                    round_act((p - 1) % CH)
                if not (isinstance(c, int) and p < 2):
                    act.wait_ge(ffn_split, n - 1)
                seed(n, bank[2 * (p % 2)][:, :], cg[:, p % 2, :], n, seed_g)
                act.wait_ge(up_v, n + 1)
                round_unit(rnd, 2)
                round_unit(rnd, 3)
                seed(n, bank[2 * (p % 2) + 1][:, :], cv[:, :], n + FT, seed_v)
                act.wait_ge(conv_g, n + 1)
                nc.scalar.activation(cg[:, p % 2, :], cg[:, p % 2, :], ACT.Gelu_apprx_tanh).then_inc(ffn_gelu, 1)

            for p in range(CH):
                pair(0, p, R_FFN + p + 1)
            with act.Fori(1, NCH) as c:
                r0 = c * 6 + R_FFN - 2
                pair(c, 0, r0 + 1)
                for j in range(4):
                    act.wait_ge(down_done, c * KT + 4 * j + 4 - KT)
                    round_unit(r0 + 2 + j // 2, 2 * (j % 2))
                    round_unit(r0 + 2 + j // 2, 2 * (j % 2) + 1)
                for p in range(1, CH):
                    pair(c, p, r0 + 3 + p)
            act.wait_ge(ffn_prod, FT)
            round_act(CH - 1)
            act.wait_ge(ffn_split, FT)
            act.wait_ge(down_done, (NCH - 1) * KT + 4)
            round_unit(ROUNDS - 1, 0)
            round_unit(ROUNDS - 1, 1)
            act.wait_ge(down_done, (NCH - 1) * KT + 8)
            round_unit(ROUNDS - 1, 2)
            round_unit(ROUNDS - 1, 3)
            for m in range(KT):
                act.wait_ge(down_added, (NCH - 1) * KT + m + 1)
                square(cg[:, m % 2, :], tile(acc, m), m + 3 * KT)
            std(4, ss2[:, :])

        @block.tensor
        def _(pe):
            def three(out, w, w_l, v, v_l, start, stop):
                nc.tensor.matmul(out, w, v, start=start, stop=False)
                nc.tensor.matmul(out, w, v_l, start=False, stop=False)
                return nc.tensor.matmul(out, w_l, v, start=False, stop=stop)

            def unit(s, j):
                return w_hi[:, s, P * j:P * j + P], w_lo[:, s, P * j:P * j + P]

            def token_totals(ss, b):
                nc.tensor.matmul(b[:, 0:ss.shape[-1]], ones, ss, start=True, stop=True).then_inc(totals, 1)

            def ada_half(c, half):
                for q in range(8):
                    s = q % RING
                    pe.wait_ge(raw_in[s], c * 64 + 32 * half + 16 * (q // RING) + 16)
                    for i in range(2):
                        k = 2 * q + i
                        mm = nc.tensor.matmul(bank[half][0:2, :], csil[:, 2 * k:2 * k + 2], w_raw[:, s, 512 * i:512 * i + 512],
                                              start=k == 0, stop=k == KT - 1)
                    mm.then_inc(ada0_used, 1)

            def turn(c):
                pe.wait_ge(rows_copied, c * 2 + 2)
                if not (isinstance(c, int) and c == 0):
                    pe.wait_ge(mod_made, c)
                for half in range(2):
                    for j in range(4):
                        mm = nc.tensor.matmul(bank[5][:, 8 * half + 2 * j:8 * half + 2 * j + 2],
                                              sq0[0:2, half, P * j:P * j + P], ident[0:2, 0:2], start=True, stop=True)
                mm.then_inc(turned, 1)

            pe.wait_ge(csil_done, 1)
            ada_half(0, 0)
            ada_half(0, 1)
            pe.wait_ge(sq_added, KT)
            token_totals(ss_x[:, :], bank[6])
            pe.wait_ge(sq_added, 2 * KT)
            token_totals(ss_c[:, :], bank[7])
            with pe.Fori(1, NADA) as c:
                pe.wait_ge(rows_copied, c * 2 - 1)
                ada_half(c, 0)
                turn(c - 1)
                ada_half(c, 1)
            turn(NADA - 1)

            def half_job(out, rnd, s, half, ready=None):
                pe.wait_ge(lo_done, rnd * RING + s + half + 1)
                for j in range(8):
                    k = 8 * half + j
                    if ready is not None:
                        pe.wait_ge(*ready(k))
                    w, w_l = unit(s + half, j)
                    mm = three(out, w, w_l, h_hi[:, k, :], h_lo[:, k, :], k == 0, k == KT - 1)
                return mm

            def job(out, rnd, s, ready=None):
                for half in range(2):
                    mm = half_job(out, rnd, s, half, ready)
                return mm

            def sum_ada(n, b):
                pe.wait_ge(ada_eaten, n * BGU + BGU)
                for j in range(2):
                    mm = nc.tensor.matmul(b[:, j:j + 1], ada_acc[:, P * j:P * j + P], ones[:, 0:1], start=True, stop=True)
                mm.then_inc(ada_summed, 1)

            def head(h):
                first = isinstance(h, int)
                for half in range(2):
                    pe.wait_ge(lo_done, h * RING + half + 1)
                    for j in range(8):
                        k = 8 * half + j
                        if first:
                            pe.wait_ge(h_ready, k + 1)
                        w, w_l = unit(half, j)
                        three(bank[0][:, :], w, w_l, h_hi[:, k, :], h_lo[:, k, :], k == 0, k == KT - 1)
                        mm = three(bank[2][:, 0:C], w, w_l, hc_hi[:, k, :], hc_lo[:, k, :], k == 0, k == KT - 1)
                mm.then_inc(ux_done, 1)
                if not first:
                    pe.wait_ge(gates_read, h * 2)
                sum_ada(h, bank[5])
                mm = job(bank[1][:, :], h, 2)
                mm.then_inc(ug_done, 1)
                pe.wait_ge(xc_split, h + 1)
                pe.wait_ge(gate_lo, h + 1)
                pe.wait_ge(ada_read, h + 1)
                for d in range(2):
                    xb, cb = GATE_BANKS[d]
                    w2 = [(g_hi[:, P * j:P * j + P], g_lo[:, P * j:P * j + P]) for j in (2 * d, 2 * d + 1)]
                    for t, (w, w_l) in enumerate(w2):
                        three(bank[xb + t][:, :], w, w_l, xc_hi[:, C:C + L], xc_lo[:, C:C + L], True, True)
                    if d == 1:
                        pe.wait_ge(gelu_done, h + 1)
                    for t, (w, w_l) in enumerate(w2):
                        mm = three(bank[cb][:, C * t:C * t + C], w, w_l, xc_hi[:, 0:C], xc_lo[:, 0:C], True, True)
                    mm.then_inc(gates_done, 1)

            head(0)
            with pe.Fori(1, HEADS) as h:
                head(h)

            def weights_dft(g):
                pe.wait_ge(tab_lo, g + 5)
                if not isinstance(g, int):
                    pe.wait_ge(m_split, g * 2)
                for t in range(2):
                    for cs in range(2):
                        for j in range(2):
                            at = slice(GW * j + P * t, GW * j + P * t + P)
                            mm = three(bank[6 + t][:, GW * cs:GW * cs + GW], chan_hi[:, cs, at], chan_lo[:, cs, at],
                                       wf_hi[:, j, :], wf_lo[:, j, :], j == 0, j == 1)
                mm.then_inc(m_done, 1)

            def channel_mix(g):
                pe.wait_ge(eo_split, g * 2 + 2)
                pe.wait_ge(m_split, g * 2 + 2)
                for dt in range(2):
                    for t in range(2):
                        for i, m in enumerate((m_hi, m_lo)):
                            mm = nc.tensor.matmul(bank[2][:, 2 * dt:2 * dt + 2], m[:, t, P * dt:P * dt + P], nyq[:, t, :],
                                                  start=(t == 0 and i == 0), stop=(t == 1 and i == 1))
                mm.then_inc(nyq_done, 1)
                for cs in range(2):
                    for nt in range(2):
                        for t in range(2):
                            at = slice(P * nt, P * nt + P)
                            mm = three(bank[4 + cs][:, GW * nt:GW * nt + GW], eo_hi[:, t, cs, at], eo_lo[:, t, cs, at],
                                       m_hi[:, t, GW * cs:GW * cs + GW], m_lo[:, t, GW * cs:GW * cs + GW], t == 0, t == 1)
                mm.then_inc(p_done, 1)

            def token_dft(g, g_next=True):
                pe.wait_ge(p_split, g * 2 + 2)
                pe.wait_ge(nyq_read, g + 1)
                pe.wait_ge(m_split, g * 2 + (4 if g_next else 2))
                for dt in range(2):
                    for cs in range(2):
                        out = bank[(2, 6)[dt] + cs]
                        for nt in range(2):
                            at = slice(GW * nt + P * dt, GW * nt + P * dt + P)
                            f = slice(NFREQ * nt, NFREQ * nt + NFREQ)
                            mm = three(out[:, 0:NFREQ], p_hi[:, cs, at], p_lo[:, cs, at],
                                       tok_hi[:, cs, f], tok_lo[:, cs, f], nt == 0, nt == 1)
                mm.then_inc(yf_done, 1)

            def fourier_tile(g, t):
                job(bank[t][:, :], g + R_FOUR, 2 * t).then_inc(uf_done, 1)

            fourier_tile(0, 0)
            pe.wait_ge(gates_read, 2 * HEADS)
            sum_ada(HEADS, bank[3])
            fourier_tile(0, 1)
            weights_dft(0)
            sum_ada(HEADS + 1, bank[4])
            with pe.Fori(1, GROUPS) as g:
                pe.wait_ge(uf_copied, g * 2 - 1)
                fourier_tile(g, 0)
                pe.wait_ge(ada_read, g * 2 + HEADS)
                sum_ada(g * 2 + HEADS, bank[3])
                channel_mix(g - 1)
                weights_dft(g)
                pe.wait_ge(uf_copied, g * 2)
                fourier_tile(g, 1)
                pe.wait_ge(ada_read, g * 2 + HEADS + 1)
                token_dft(g - 1)
                sum_ada(g * 2 + HEADS + 1, bank[4])
            pe.wait_ge(ada_read, HEADS + 2 * GROUPS)
            channel_mix(GROUPS - 1)

            pe.wait_ge(uf_copied, 2 * GROUPS)
            half_job(bank[0][:, :], R_OUT, 0, 0, lambda k: (yc_ready, k + 1))
            token_dft(GROUPS - 1, False)
            half_job(bank[1][:, :], R_OUT, 2, 0)
            half_job(bank[0][:, :], R_OUT, 0, 1, lambda k: (yc_ready, k + 1)).then_inc(y_done, 1)
            half_job(bank[1][:, :], R_OUT, 2, 1).then_inc(y_done, 1)
            AT_OUT = HEADS + 2 * GROUPS
            sum_ada(AT_OUT, bank[3])
            with pe.Fori(1, KT // 2) as i:
                for t in range(2):
                    pe.wait_ge(sq_done, i * 2 + t - 1 + 2 * KT)
                    job(bank[t][:, :], i + R_OUT, 2 * t).then_inc(y_done, 1)
                    pe.wait_ge(ada_read, i * 2 + AT_OUT - 1 + t)
                    sum_ada(i * 2 + AT_OUT - 1 + t, bank[3])
            pe.wait_ge(sq_added, 3 * KT)
            token_totals(ss1[:, :], bank[6])
            for k in range(KT):
                pe.wait_ge(x1_squared, k + 1)
                nc.tensor.matmul(bank[5][:, :], ones, sq1[:, k % 2, :], start=k == 0,
                                 stop=k == KT - 1).then_inc(x1_summed if k < KT - 1 else totals, 1)

            def up_pair(c, p, rnd, ready=None):
                n = c * CH + p
                if not (isinstance(c, int) and c == 0 and p < 2):
                    pe.wait_ge(conv_v, n - 1)
                b = 2 * (p % 2)
                job(bank[b][:, :], rnd, 0, ready).then_inc(up_g, 1)
                job(bank[b + 1][:, :], rnd, 2).then_inc(up_v, 1)

            def down(c, rnd):
                pe.wait_ge(ffn_split, c * CH + CH)
                for m in range(KT):
                    s, u = m // 2 % RING, m // 2
                    if m % 2 == 0:
                        pe.wait_ge(lo_done, rnd * RING + u + 1)
                    if not (isinstance(c, int) and c == 0 and m < 4):
                        pe.wait_ge(down_added, c * KT + m - 3)
                    for k in range(CH):
                        w, w_l = unit(s, CH * (m % 2) + k)
                        mm = three(bank[4 + m % 4][:, :], w, w_l, act_hi[:, k, :], act_lo[:, k, :], k == 0, k == CH - 1)
                    mm.then_inc(down_done, 1)

            for p in range(CH):
                up_pair(0, p, R_FFN + p, (lambda k: shared(h2_ready, POOL_H2, k)) if p == 0 else None)
                if p == 0:
                    sum_ada(LAST_ADA, bank[4])
            up_pair(1, 0, R_FFN + CH)
            pe.wait_ge(ada_read, NBG)
            down(0, R_FFN + CH + 1)
            for p in range(1, CH):
                up_pair(1, p, R_FFN + CH + 2 + p)
            with pe.Fori(2, NCH) as c:
                r0 = c * 6 + R_FFN - 2
                up_pair(c, 0, r0)
                down(c - 1, r0 + 1)
                for p in range(1, CH):
                    up_pair(c, p, r0 + 2 + p)
            down(NCH - 1, ROUNDS - 2)
            pe.wait_ge(sq_added, 4 * KT)
            token_totals(ss2[:, :], bank[0])

        @block.vector
        def _(dve):
            chain = Chain(dve, dve_chain)
            v = nc.vector

            def add_positions(x, tables, n):
                for i in range(4):
                    dve.wait_ge(x_in[i], 16 * n + 16)
                    piece = x[:, 4 * i:4 * i + 4, :].rearrange("p k (r c) -> p k r c", c=GRID)
                    if i < 2:
                        pos = lcol(tables, "row_pos", 32 * i, 32).rearrange("p (k r o) -> p k r o", k=4, o=1)
                    else:
                        pos = lcol(tables, "col_pos", 4 * GRID * (i - 2), 4 * GRID).rearrange("p (k o c) -> p k o c", k=4, o=1)
                    v.tensor_tensor(piece, piece, pos.broadcast_to([P, 4, L // GRID, GRID]), ALU.add).then_inc(x_posed, 1)

            def add_square(ss, sq, n, first=False):
                dve.wait_ge(sq_done, n + 1)
                if first:
                    v.tensor_copy(ss, sq).then_inc(sq_added, 1)
                else:
                    dve.wait_ge(sq_added, n)
                    v.tensor_tensor(ss, ss, sq, ALU.add).then_inc(sq_added, 1)

            def inverse_rms(n, b, rms):
                dve.wait_ge(totals, n + 1)
                v.tensor_scalar(rms, b[:, 0:rms.shape[-1]], 1.0 / D, EPS, ALU.mult, ALU.add).then_inc(var_done, 1)
                dve.wait_ge(std_done, n + 1)
                v.reciprocal(rms, rms).then_inc(rms_done, 1)
                dve.wait_ge(rms_done, n + 1)

            def take_ada(n, b):
                dve.wait_ge(ada_summed, n + 1)
                at = n * 2 + 2 * KT
                v.tensor_tensor(mod_x[:, ds(at, 2)], b[:, 0:2], pcol("b_ada", at, 2), ALU.add).then_inc(ada_read, 1)

            def eat_ada(n, q0, q1):
                for q in range(q0, q1):
                    dve.wait_ge(ada_in[q % ASLOTS], n * (16 * BGU // ASLOTS) + 16 * (q // ASLOTS) + 16)
                    for i in range(2):
                        k = 2 * q + i
                        rows, scale = ada_raw[:, q % ASLOTS, ACOL * i:ACOL * i + ACOL], csil[:, 2 * k:2 * k + 1]
                        if k == 0:
                            ins = v.tensor_scalar(ada_acc[:, :], rows, scale, None, ALU.mult)
                        else:
                            if i == 0:
                                dve.wait_ge(ada_eaten, n * BGU + q)
                            else:
                                chain.wait()
                            ins = v.scalar_tensor_tensor(ada_acc[:, :], rows, scale, ada_acc[:, :], ALU.mult, ALU.add)
                        if i == 0:
                            chain.step(ins)
                        else:
                            ins.then_inc(ada_eaten, 1)

            t1, t2, t3 = (small[:, 96 + 16 * i:112 + 16 * i] for i in range(3))
            dve.wait_ge(csig_done, 1)
            v.tensor_tensor(csil[:, :], csil[:, :], pcol("cond"), ALU.mult).then_inc(csil_done, 1)
            dve.wait_ge(exp_lam, 1)
            chain.step(v.tensor_scalar(t1, decay[:, 1, :], 2.0, None, ALU.add))
            chain.wait()
            chain.step(v.reciprocal(t2, t1))
            chain.wait()
            chain.step(v.tensor_tensor(t1, decay[:, 1, :], t2, ALU.mult))
            chain.wait()
            chain.step(v.tensor_tensor(t2, t1, t1, ALU.mult))
            chain.wait()
            chain.step(v.tensor_scalar(t3, t2, 1.0 / 17, None, ALU.mult))
            for odd in (15, 13, 11, 9, 7, 5, 3):
                chain.wait()
                chain.step(v.scalar_tensor_tensor(t3, t3, 1.0 / odd, t2, ALU.add, ALU.mult))
            chain.wait()
            chain.step(v.scalar_tensor_tensor(t1, t3, 1.0, t1, ALU.add, ALU.mult))
            chain.step(v.tensor_scalar(t2, pcol("lam"), -1.0, 0.0, ALU.mult, ALU.max))
            chain.wait()
            chain.step(v.scalar_tensor_tensor(t3, t1, 2.0, t2, ALU.mult, ALU.add))
            chain.wait()
            chain.step(v.tensor_scalar(decay[:, 1, :], t3, 4.0, None, ALU.mult))
            v.tensor_scalar(decay[:, 2, :], t3, -8.0, None, ALU.mult).then_inc(decay_done, 1)

            dve.wait_ge(pos_in, 16)
            add_positions(x0, pos0, 0)
            for k in range(KT):
                add_square(ss_x[:, :], sq0[:, k % 2, :], k, first=(k == 0))
            for k in range(KT):
                add_square(ss_c[:, :], sq0[:, k % 2, 0:C], KT + k, first=(k == 0))
            inverse_rms(0, bank[6], ss_x[:, :])
            inverse_rms(1, bank[7], ss_c[:, :])

            def part(t, c):
                return t[:, 0:2 * KT].rearrange("p (h k) -> p h k", h=2)[:, :, 4 * c:4 * c + 4]

            for c in range(NADA):
                dve.wait_ge(turned, c + 1)
                both = bank[5][:, 0:16].rearrange("p (h b c) -> p h b c", h=2, c=2)
                chain.step(v.tensor_tensor(part(mod_x, c), both[:, :, :, 0], part(pcol("b_ada"), c), ALU.add))
                v.tensor_tensor(part(mod_c, c), both[:, :, :, 1], part(pcol("b_ada"), c), ALU.add).then_inc(mod_made, 1)
                chain.wait()
                dve.wait_ge(mod_made, c + 1)
                for g, m in ((gain_x, mod_x), (gain_c, mod_c)):
                    chain.step(v.scalar_tensor_tensor(g[:, 4 * c:4 * c + 4], m[:, KT + 4 * c:KT + 4 * c + 4], 1.0,
                                                      pcol("g_mix_pre", 4 * c, 4), ALU.add, ALU.mult))
                chain.wait()
                for k in range(4 * c, 4 * c + 5):
                    if k < 4 * c + 4:
                        v.scalar_tensor_tensor(x0[:, k, :], x0[:, k, :], gain_x[:, k:k + 1], ss_x[:, :],
                                               ALU.mult, ALU.mult).then_inc(h_pre, 1)
                        v.scalar_tensor_tensor(c0[:, k, :], c0[:, k, :], gain_c[:, k:k + 1], ss_c[:, :],
                                               ALU.mult, ALU.mult).then_inc(h_pre, 1)
                    if k > 4 * c:
                        j = k - 1
                        dve.wait_ge(h_rounded, 2 * j + 2)
                        v.scalar_tensor_tensor(h_lo[:, j, :], x0[:, j, :], mod_x[:, j:j + 1], h_hi[:, j, :].bitcast(F32),
                                               ALU.add, ALU.subtract)
                        v.scalar_tensor_tensor(hc_lo[:, j, :], c0[:, j, :], mod_c[:, j:j + 1], hc_hi[:, j, :].bitcast(F32),
                                               ALU.add, ALU.subtract).then_inc(h_ready, 1)

            def convolve(h):
                segments = ((bank[0], C, L), (bank[2], 0, C))
                dve.wait_ge(xc_seed, h * 2 + 2)
                for tap, off in ((0, -2), (1, -1), (3, 1)):
                    w = pcol("lru_conv_w", h * 4 + tap, 1)
                    for b, at, n in segments:
                        lo, hi = max(0, -off), min(n, n - off)
                        dst = xc[:, at + lo:at + hi]
                        if tap:
                            chain.wait()
                        ins = v.scalar_tensor_tensor(dst, b[:, lo + off:hi + off], w, dst, ALU.mult, ALU.add)
                        if tap == 3 and at == 0:
                            ins.then_inc(xc_done, 1)
                        else:
                            chain.step(ins)

            def finish_head(h):
                for d in range(2):
                    dve.wait_ge(root_done, h * 2 + d + 1)
                    chain.step(v.tensor_tensor(lru_i[:, d, :], lru_i[:, d, :], lru_u[:, d, :], ALU.mult))
                    chain.wait()
                    if d == 0:
                        ins = v.tensor_tensor_scan(lru_u[:, d, :], lru_r[:, d, :], lru_i[:, d, :], 0.0, ALU.mult, ALU.add)
                    else:
                        a, b, o = (t[:, d, C - 1::-1] for t in (lru_r, lru_i, lru_u))
                        chain.step(v.tensor_tensor_scan(o, a, b, 0.0, ALU.mult, ALU.add))
                        chain.wait()
                        a, b, o = (t[:, d, C + L - 1:C - 1:-1] for t in (lru_r, lru_i, lru_u))
                        ins = v.tensor_tensor_scan(o, a, b, lru_u[:, d, 0:1], ALU.mult, ALU.add)
                    ins.then_inc(scan_done, 1)
                dve.wait_ge(scan_done, h * 2 + 2)
                chain.step(v.tensor_tensor(lru_u[:, 0, C:C + L], lru_u[:, 0, C:C + L], lru_u[:, 1, C:C + L], ALU.add))
                chain.wait()
                dve.wait_ge(gelu_done, h + 1)
                v.tensor_tensor(tile(y_lru, h), tile(y_lru, h), lru_u[:, 0, C:C + L], ALU.mult).then_inc(head_done, 1)

            def head(h):
                first = isinstance(h, int)
                dve.wait_ge(gate_hi, h + 1)
                v.tensor_tensor(g_lo[:, :], g_raw[:, :], g_hi[:, :].bitcast(F32), ALU.subtract).then_inc(gate_lo, 1)
                if first:
                    eat_ada(0, 0, BGU)
                convolve(h)
                dve.wait_ge(xc_round, h + 1)
                v.tensor_tensor(xc_lo[:, :], xc[:, :], xc_hi[:, :].bitcast(F32), ALU.subtract).then_inc(xc_split, 1)
                take_ada(h, bank[5])
                if not first:
                    finish_head(h - 1)
                eat_ada(h + 1, 0, BGU)
                dve.wait_ge(gates_read, h * 2 + 2)
                for d in range(2):
                    chain.step(v.tensor_tensor(lru_i[:, d, :], lru_i[:, d, :], xc[:, :], ALU.mult))
                for d in range(2):
                    dve.wait_ge(exp_done, h * 2 + d + 1)
                    chain.step(v.scalar_tensor_tensor(lru_u[:, d, :], lru_r[:, d, :], 1.0, lru_u[:, d, :], ALU.add, ALU.mult))
                    chain.wait()
                    chain.step(v.tensor_scalar(lru_r[:, d, :], lru_u[:, d, :], -1.0, 1.0, ALU.mult, ALU.add))
                    chain.wait()
                    v.scalar_tensor_tensor(lru_u[:, d, :], lru_r[:, d, :], 1.0, lru_u[:, d, :],
                                           ALU.add, ALU.mult).then_inc(gap_done, 1)

            head(0)
            with chain.loop(1, HEADS, 5 + 4 + 8 + 2 + 4) as h:
                head(h)
            finish_head(HEADS - 1)

            def split_table(n, hi, lo, src):
                dve.wait_ge(tab_hi, n + 1)
                v.tensor_tensor(lo, src[:, 0:hi.shape[-1]], hi.bitcast(F32), ALU.subtract).then_inc(tab_lo, 1)

            def fourier_input(g, t):
                n = g * 2 + t
                dve.wait_ge(uf_copied, n + 1)
                if not (isinstance(g, int) and t == 0):
                    dve.wait_ge(eo_split, n)
                if not isinstance(g, int) and t == 0:
                    chain.wait()
                u, rev = u_sb[:, 1:C], u_sb[:, L - 1:C:-1]
                chain.step(v.tensor_tensor(eo[:, 0, 1:C], u, rev, ALU.add))
                chain.step(v.tensor_tensor(eo[:, 1, 1:C], u, rev, ALU.subtract))
                v.tensor_copy(eo[:, 0, 0:1], u_sb[:, 0:1]).then_inc(eo_done, 1)
                dve.wait_ge(eo_rounded, n + 1)
                chain.step(v.tensor_tensor(nyq[:, t, 1:2], u_sb[:, C:C + 1], nyq[:, t, 0:1].bitcast(F32), ALU.subtract))
                v.tensor_tensor(eo_lo[:, t, :, :], eo[:, :, :], eo_hi[:, t, :, :].bitcast(F32), ALU.subtract).then_inc(eo_split, 1)

            def split_m(g):
                for t in range(2):
                    dve.wait_ge(m_rounded, g * 2 + t + 1)
                    v.tensor_tensor(m_lo[:, t, :], bank[6 + t][:, :], m_hi[:, t, :].bitcast(F32), ALU.subtract).then_inc(m_split, 1)

            def split_p(g):
                for t in range(2):
                    dve.wait_ge(p_rounded, g * 2 + t + 1)
                    v.tensor_tensor(p_lo[:, t, :], bank[4 + t][:, :], p_hi[:, t, :].bitcast(F32), ALU.subtract).then_inc(p_split, 1)

            def read_nyq(g):
                dve.wait_ge(nyq_done, g + 1)
                v.tensor_copy(nyq_p[:, 0:4], bank[2][:, 0:4]).then_inc(nyq_read, 1)
                dve.wait_ge(nyq_read, g + 1)
                two = nyq_p[:, 0:4].rearrange("p (d c) -> p d c", c=2)
                chain.step(v.tensor_tensor(nyq_p[:, 4:6], two[:, :, 0], two[:, :, 1], ALU.add))
                chain.wait()
                bias = pcol("b_fourier", g * 2, 2)
                chain.step(v.tensor_tensor(nyq_p[:, 6:8], bias, nyq_p[:, 4:6], ALU.add))
                chain.step(v.tensor_tensor(nyq_p[:, 8:10], bias, nyq_p[:, 4:6], ALU.subtract))

            def fourier_output(g, g_next=True):
                dve.wait_ge(yf_done, g + 1)
                cosine = eo[:, :, :].rearrange("p t c -> p (t c)")
                dve.wait_ge(eo_split, g * 2 + (4 if g_next else 2))
                for dt in range(2):
                    a, b = bank[(2, 6)[dt]], bank[(3, 7)[dt]]
                    chain.wait()
                    for odd in range(2):
                        chain.step(v.tensor_scalar(cosine[:, odd:NFREQ:2], a[:, odd:NFREQ:2],
                                                   nyq_p[:, 6 + 2 * odd + dt:7 + 2 * odd + dt], None, ALU.add))
                    chain.wait()
                    n = g * 2 + dt
                    v.tensor_tensor(tile(y_four, n, 0, C), cosine[:, 0:C], b[:, 0:C], ALU.subtract)
                    chain.step(v.tensor_copy(tile(y_four, n, C, C + 1), cosine[:, C:C + 1]))
                    last = v.tensor_tensor(tile(y_four, n, C + 1, L), cosine[:, C - 1:0:-1], b[:, C - 1:0:-1], ALU.add)
                    if dt == 0:
                        chain.step(last)
                last.then_inc(yf_read, 1)
                clear_odd()

            def clear_odd():
                chain.wait()
                chain.step(v.memset(eo[:, 1, 0:1], 0.0))

            dve.wait_ge(head_done, HEADS)
            clear_odd()
            fourier_input(0, 0)
            for n in range(4):
                hi, lo = (chan_hi, chan_lo) if n < 2 else (tok_hi, tok_lo)
                split_table(n, hi[:, n % 2, :], lo[:, n % 2, :], y_four[:, ds(n * 2 * NFREQ, 2 * NFREQ)])
            wf_all = tuple(t[:, :, :].rearrange("p t d -> p (t d)") for t in (wf_hi, wf_lo))
            split_table(4, *wf_all, tab_raw)
            take_ada(HEADS, bank[3])
            eat_ada(HEADS + 1, 0, BGU)
            fourier_input(0, 1)
            split_m(0)
            take_ada(HEADS + 1, bank[4])
            with chain.loop(1, GROUPS, 16 + 6 + 3 + 8) as g:
                eat_ada(g * 2 + HEADS, 0, BGU)
                split_table(g + 4, *wf_all, tab_raw)
                fourier_input(g, 0)
                take_ada(g * 2 + HEADS, bank[3])
                read_nyq(g - 1)
                split_p(g - 1)
                split_m(g)
                eat_ada(g * 2 + HEADS + 1, 0, BGU)
                fourier_input(g, 1)
                fourier_output(g - 1)
                take_ada(g * 2 + HEADS + 1, bank[4])

            def split_ycat(n, src):
                dve.wait_ge(yc_rounded, n + 1)
                v.tensor_tensor(h_lo[:, n, :], src, h_hi[:, n, :].bitcast(F32), ALU.subtract).then_inc(yc_ready, 1)

            for n in range(4):
                split_ycat(n, tile(y_lru, n))
            read_nyq(GROUPS - 1)
            split_p(GROUPS - 1)
            for n in range(4, HEADS):
                split_ycat(n, tile(y_lru, n))
            fourier_output(GROUPS - 1, False)
            for n in range(8):
                split_ycat(HEADS + n, tile(y_four, n))

            AT_OUT = HEADS + 2 * GROUPS

            def out_tiles(i, ada=2):
                for t in range(2):
                    m = i * 2 + t
                    first = isinstance(i, int) and m == 0
                    if first:
                        eat_ada(AT_OUT, 0, BGU)
                    add_square(ss1[:, :], sq1[:, t, :], m + 2 * KT, first=first)
                    if not first:
                        take_ada(m + AT_OUT - 1, bank[3])
                        if t < ada:
                            eat_ada(m + AT_OUT, 0, BGU)

            out_tiles(0)
            with chain.loop(1, 4, 16) as i:
                out_tiles(i)
            dve.wait_ge(late_in, 16)
            add_positions(x1, late_par, 1)
            with chain.loop(4, KT // 2 - 1, 16) as i:
                out_tiles(i)
            chain.step(v.tensor_tensor(gain_y, mod_x[:, 2 * KT:3 * KT], pcol("g_mix_post"), ALU.mult))
            out_tiles(KT // 2 - 1, 1)
            dve.wait_ge(ada_read, LAST_ADA)
            chain.step(v.scalar_tensor_tensor(gain_f, mod_x[:, 4 * KT:5 * KT], 1.0, pcol("g_ffn_pre"), ALU.add, ALU.mult))
            inverse_rms(2, bank[6], ss1[:, :])
            for k in range(KT):
                ins = v.scalar_tensor_tensor(tile(acc, k), tile(acc, k), gain_y[:, k:k + 1], ss1[:, :], ALU.mult, ALU.mult)
                if k in POOL_SUM:
                    ins.then_inc(y_normed, 1)
                else:
                    chain.step(ins)
                    chain.wait()
                    v.tensor_tensor(x1[:, k, :], x1[:, k, :], tile(acc, k), ALU.add).then_inc(x1_done[0], 1)
            dve.wait_ge(y_normed, len(POOL_SUM))
            inverse_rms(3, bank[5], ss1[:, :])
            mine = [k for k in range(KT) if k not in POOL_H2]
            for n in range(len(mine) + 1):
                if n < len(mine):
                    k = mine[n]
                    v.scalar_tensor_tensor(tile(acc, k), x1[:, k, :], gain_f[:, k:k + 1], ss1[:, :],
                                           ALU.mult, ALU.mult).then_inc(h2_pre[0], 1)
                if n > 0:
                    k = mine[n - 1]
                    dve.wait_ge(h2_rounded[0], n)
                    v.scalar_tensor_tensor(h_lo[:, k, :], tile(acc, k), mod_x[:, 3 * KT + k:3 * KT + k + 1],
                                           h_hi[:, k, :].bitcast(F32), ALU.add, ALU.subtract).then_inc(h2_ready[0], 1)
            eat_ada(LAST_ADA, 0, BGU)

            def convolve_ffn(b, dst, tile_no, done):
                chain.step(v.scalar_tensor_tensor(dst[:, 1:L], b[:, 0:L - 1], lcol(late_par, "ffn_conv_w", tile_no * 3, 1), dst[:, 1:L],
                                                  ALU.mult, ALU.add))
                chain.wait()
                v.scalar_tensor_tensor(dst[:, 0:L - 1], b[:, 1:L], lcol(late_par, "ffn_conv_w", tile_no * 3 + 2, 1), dst[:, 0:L - 1],
                                       ALU.mult, ALU.add).then_inc(done, 1)

            def split_act(n, q):
                dve.wait_ge(ffn_round, n + 1)
                v.tensor_tensor(act_lo[:, q, :], cg[:, q % 2, :], act_hi[:, q, :].bitcast(F32), ALU.subtract).then_inc(ffn_split, 1)

            def pair(c, p):
                n = c * CH + p
                if not (isinstance(c, int) and n == 0):
                    split_act(n - 1, (p - 1) % CH)
                dve.wait_ge(seed_g, n + 1)
                convolve_ffn(bank[2 * (p % 2)], cg[:, p % 2, :], n, conv_g)
                dve.wait_ge(seed_v, n + 1)
                convolve_ffn(bank[2 * (p % 2) + 1], cv[:, :], n + FT, conv_v)
                dve.wait_ge(conv_v, n + 1)
                dve.wait_ge(ffn_gelu, n + 1)
                v.tensor_tensor(cg[:, p % 2, :], cg[:, p % 2, :], cv[:, :], ALU.mult).then_inc(ffn_prod, 1)

            def add_down(c, m):
                dve.wait_ge(down_done, c * KT + m + 1)
                if isinstance(c, int) and c == 0:
                    v.tensor_copy(tile(acc, m), bank[4 + m % 4][:, :]).then_inc(down_added, 1)
                else:
                    v.tensor_tensor(tile(acc, m), tile(acc, m), bank[4 + m % 4][:, :], ALU.add).then_inc(down_added, 1)

            def chunk(c):
                pair(c, 0)
                for m in range(KT):
                    add_down(c - 1, m)
                for p in range(1, CH):
                    pair(c, p)

            for p in range(CH):
                pair(0, p)
                if p == 0:
                    take_ada(LAST_ADA, bank[4])
                    dve.wait_ge(ada_read, NBG)
                    chain.step(v.tensor_tensor(gain_d, mod_x[:, 5 * KT:6 * KT], pcol("g_ffn_post"), ALU.mult))
            chunk(1)
            with chain.loop(2, NCH, 2 * CH) as c:
                chunk(c)
            split_act(FT - 1, CH - 1)
            for m in range(KT):
                add_down(NCH - 1, m)
                for j in range(2 * m - KT, 2 * m - KT + 2):
                    if j >= 0:
                        add_square(ss2[:, :], cg[:, j % 2, :], j + 3 * KT, first=(j == 0))
            inverse_rms(4, bank[0], ss2[:, :])
            for k in range(KT):
                ins = v.scalar_tensor_tensor(tile(acc, k), tile(acc, k), gain_d[:, k:k + 1], ss2[:, :], ALU.mult, ALU.mult)
                if k in POOL_SUM:
                    ins.then_inc(f_normed, 1)
                else:
                    chain.step(ins)
                    chain.wait()
                    v.tensor_tensor(x1[:, k, :], x1[:, k, :], tile(acc, k), ALU.add).then_inc(out_ready[0], 1)


def dft_tables():
    j, c = np.arange(GW)[:, None], np.arange(GW)[None, :]
    turn = 2 * np.pi * ((j * c) % GW) / GW
    scale = 1 / np.sqrt(L * GW)
    n, k = np.arange(L // 2)[:, None], np.arange(NFREQ)[None, :]
    turn_tok = 2 * np.pi * ((n * k) % L) / L
    sines = np.sin(turn_tok)
    sines[(2 * n * k) % L == 0] = 0.0
    out = np.zeros((4, P, 2 * NFREQ), np.float32)
    for t, table in enumerate((np.cos(turn) * scale, np.sin(turn) * scale, np.cos(turn_tok), sines)):
        width = 2 * table.shape[1]
        out[t, :, :width] = table.reshape(2, P, -1).transpose(1, 0, 2).reshape(P, width)
    return out


def position_tables():
    quarter = D // 4
    freqs = np.float32(10000.0) ** (-np.arange(quarter, dtype=np.float32) / np.float32(quarter))
    out = []
    for n in (L // GRID, GRID):
        angle = (np.arange(n, dtype=np.float32)[:, None] * freqs[None, :]).astype(np.float64)
        enc = np.concatenate([np.sin(angle), np.cos(angle)], axis=-1).astype(np.float32)
        out.append(enc.T)
    return out


def columns(a):
    a = a.reshape(-1, P, *a.shape[1:])
    return np.moveaxis(a, 1, 0).reshape(P, -1)


def kernel(**inputs):
    import concourse.bacc as bacc
    from concourse.bass_utils import run_bass_kernel_spmd

    a = {k: np.asarray(val) for k, val in inputs.items()}
    w = {k: a[k][0] for k in a if k not in ("x", "c", "ctx", "c_ctx")}

    def feature_tiles(x):
        return np.ascontiguousarray(x.T.reshape(KT, P, -1).transpose(1, 0, 2))

    def units16(m):
        return m.reshape(2, 8, P, -1, P).transpose(3, 0, 2, 1, 4).reshape(-1, 2, P, UNIT)

    w_in = units16(w["w_in"])
    w_out = units16(np.concatenate([w["w_out"][D // 2:], w["w_out"][:D // 2]]))
    w_up = units16(w["w_up"])
    w_down = w["w_down"].reshape(NCH, CH, P, 8, 2, P).transpose(0, 3, 2, 4, 1, 5).reshape(NCH, 8, P, UNIT)
    parts = []
    for h in range(HEADS):
        parts += [w_in[8 + h], w_in[16 + h]]
    parts += [w_in[m] for m in range(8)] + [w_out[m] for m in range(KT)]
    for c in range(NCH):
        for p in range(CH):
            parts += [w_up[c * CH + p], w_up[FT + c * CH + p]]
            if p == 0 and c > 0:
                parts.append(w_down[c - 1])
    parts.append(w_down[NCH - 1])
    stream = np.concatenate(parts)
    assert stream.shape == (UNITS, P, UNIT)

    ada = w["w_ada"]
    ada0 = ada[:, :1024 * NADA].reshape(8, 2, P, 2, NADA, 512).transpose(4, 3, 0, 2, 1, 5).reshape(-1, P, 1024)
    adabg = ada[:, 1024 * NADA:].reshape(BGU, 2, P, NBG, ACOL).transpose(3, 0, 2, 1, 4).reshape(-1, P, 2 * ACOL)
    gates = np.stack([w["w_rec_gate"][0], w["w_in_gate"][0], w["w_rec_gate"][1], w["w_in_gate"][1]], axis=2)
    gates = gates.reshape(HEADS, P, 4 * P)
    wf = w["w_fourier"].reshape(GROUPS, 2, P, GW).transpose(0, 2, 1, 3).reshape(GROUPS, P, 2 * GW)
    tabs = np.concatenate([dft_tables(), np.pad(wf, ((0, 0), (0, 0), (0, 2 * NFREQ - 2 * GW)))])
    row_pos, col_pos = position_tables()
    per_head = {
        "lam": w["lru_lambda"].T,
        "lru_conv_w": w["conv_lru_w"].T,
        "gate_b": np.stack([w["b_rec_gate"][0], w["b_in_gate"][0], w["b_rec_gate"][1], w["b_in_gate"][1]], axis=1),
        "ffn_conv_w": w["conv_ffn_w"].T,
        "cond": np.stack([a["c"][0], a["c_ctx"]], axis=1),
        "row_pos": row_pos, "col_pos": col_pos,
        "ones": np.ones((P, P), np.float32), "ident": np.eye(P, dtype=np.float32),
        "lru_conv_b": w["conv_lru_b"], "ffn_conv_b": w["conv_ffn_b"],
    }
    par = np.concatenate([columns(per_head.get(n, w.get(n))) for n in PAR], axis=1)
    late = np.concatenate([columns(per_head[n]) for n in LATE], axis=1)
    assert par.shape == (P, NPAR) and late.shape == (P, NLATE)

    arrays = {"x_t": feature_tiles(a["x"][0]), "ctx_t": feature_tiles(a["ctx"][0]), "par": par, "late": late, "stream": stream, "ada0": ada0,
              "adabg": adabg, "gates": gates, "tabs": tabs}
    nc = bacc.Bacc("TRN2", target_bir_lowering=False, num_devices=1)
    arrays = {f"in_{n}": np.ascontiguousarray(val) for n, val in arrays.items()}
    args = [nc.dram_tensor(n, val.shape, F32, kind="ExternalInput").ap() for n, val in arrays.items()]
    out = nc.dram_tensor("out_t", (P, KT, L), F32, kind="ExternalOutput").ap()
    build(nc, *args, out)
    r = run_bass_kernel_spmd(nc, [arrays], core_ids=[0])
    got = np.asarray(r.results[0]["out_t"])
    return np.ascontiguousarray(got.transpose(1, 0, 2).reshape(D, L).T)[None]
```

```python
from contextlib import ExitStack, contextmanager

import numpy as np

import concourse.bass as bass
from concourse import mybir

F32 = mybir.dt.float32
F32R = mybir.dt.float32r
ALU = mybir.AluOpType
ACT = mybir.ActivationFunctionType
ds = bass.ds

P = 128
D = 2048
KT = D // P
L = 512
C = 256
GRID = 64
HEADS = 8
GROUPS = 4
GW = 256
FT = 5632 // P
CH = 4
NCH = FT // CH
RING = 4
UNIT = 8 * P
NFREQ = L // 2 + 2
EPS = 1e-6

U_HEADS = 4 * HEADS
U_FOUR = 4 * GROUPS
U_OUT = 2 * KT
U_FFN = 2 * 2 * FT + NCH * KT // 2
UNITS = U_HEADS + U_FOUR + U_OUT + U_FFN
NADA = 4
ASLOTS = 4
ACOL = 256
NBG = (6 * D - NADA * 1024) // ACOL
BGU = KT // 2
FFN_ADA = NBG - 2

PAR = {}
NPAR = 0
for _name, _n in (("ones", P), ("ident", P), ("cond", 2 * KT), ("b_ada", 6 * KT), ("g_mix_pre", KT), ("g_mix_post", KT),
                  ("g_ffn_pre", KT), ("g_ffn_post", KT), ("lam", 2 * HEADS), ("b_fourier", 8), ("lru_conv_w", 4 * HEADS),
                  ("lru_conv_b", HEADS), ("gate_b", 4 * HEADS)):
    PAR[_name] = (NPAR, _n)
    NPAR += _n
LATE = {}
NPOS = NLATE = 0
for _name, _n in (("row_pos", 8 * (L // GRID)), ("col_pos", 8 * GRID), ("ffn_conv_w", 3 * 2 * FT), ("ffn_conv_b", 2 * FT)):
    LATE[_name] = (NLATE, _n)
    NLATE += _n
    if _name == "col_pos":
        NPOS = NLATE


class Chain:

    def __init__(self, eng, sem):
        self.eng, self.sem, self.base, self.k = eng, sem, 0, 0

    def step(self, ins):
        ins.then_inc(self.sem, 1)
        self.k += 1

    def wait(self):
        self.eng.wait_ge(self.sem, self.base + self.k)

    @contextmanager
    def loop(self, start, stop, per):
        first = self.base + self.k
        with self.eng.Fori(start, stop) as i:
            self.base, self.k = (i - start) * per + first, 0
            yield i
            assert self.k == per, (self.k, per)
        self.base, self.k = first + (stop - start) * per, 0


def build(nc, x_t, ctx_t, par_d, late_d, stream, ada0, adabg, gates_d, tabs_d, out_t):
    ctx = ExitStack()
    with ctx:
        def sem(name):
            return ctx.enter_context(nc.semaphore(name))

        def sbuf(stack, name, shape, dt=F32, side=None):
            return stack.enter_context(nc.sbuf_tensor(name, shape, dt, side=side))

        par = sbuf(ctx, "par", [P, NPAR])
        h_hi = sbuf(ctx, "h_hi", [P, KT, L], F32R)
        h_lo = sbuf(ctx, "h_lo", [P, KT, L], F32R)
        w_raw = sbuf(ctx, "w_raw", [P, RING, UNIT])
        w_hi = sbuf(ctx, "w_hi", [P, RING, UNIT], F32R)
        w_lo = sbuf(ctx, "w_lo", [P, RING, UNIT], F32R)
        csil = sbuf(ctx, "csil", [P, 2 * KT])
        mod_x = sbuf(ctx, "mod_x", [P, 6 * KT])
        mod_c = sbuf(ctx, "mod_c", [P, 2 * KT])
        gain = sbuf(ctx, "gain", [P, 5 * KT])
        small = sbuf(ctx, "small", [P, 3 * KT])
        eps = sbuf(ctx, "eps", [P, 1])
        decay = sbuf(ctx, "decay", [P, 3, 2 * HEADS])

        def pcol(name, a=0, n=None):
            at, width = PAR[name]
            return par[:, ds(at + a, width if n is None else n)]

        def lcol(t, name, a=0, n=None):
            at, width = LATE[name]
            return t[:, ds(at + a, width if n is None else n)]

        def tile(t, k, a=0, b=L):
            return t[:, ds(k * L + a, b - a)]

        ones, ident = pcol("ones"), pcol("ident")
        gain_x, gain_c, gain_y, gain_f, gain_d = (gain[:, KT * i:KT * i + KT] for i in range(5))

        with ExitStack() as s:
            hc_hi = sbuf(s, "hc_hi", [P, KT, C], F32R)
            hc_lo = sbuf(s, "hc_lo", [P, KT, C], F32R)
            x0 = sbuf(s, "x0", [P, KT, L])
            c0 = sbuf(s, "c0", [P, KT, C])
            sq0 = sbuf(s, "sq0", [P, 2, L])
            ss_x = sbuf(s, "ss_x", [P, L])
            ss_c = sbuf(s, "ss_c", [P, C])
            pos0 = sbuf(s, "pos0", [P, NPOS])
            ada_rows = sbuf(s, "ada_rows", [P, 512])

        mix = ExitStack()
        ada_acc = sbuf(mix, "ada_acc", [P, ACOL], side="right")
        ada_raw = sbuf(mix, "ada_raw", [P, ASLOTS, 2 * ACOL], side="right")
        with ExitStack() as late:
            y_lru = sbuf(late, "y_lru", [P, HEADS * L], side="right")
            with ExitStack() as s:
                sbuf(s, "hc_hi_kept", [P, KT, C])
                sbuf(s, "hc_lo_kept", [P, KT, C])
                xc = sbuf(s, "xc", [P, C + L])
                xc_hi = sbuf(s, "xc_hi", [P, C + L], F32R)
                xc_lo = sbuf(s, "xc_lo", [P, C + L], F32R)
                lru_r = sbuf(s, "lru_r", [P, 2, C + L])
                lru_i = sbuf(s, "lru_i", [P, 2, C + L])
                lru_u = sbuf(s, "lru_u", [P, 2, C + L])
                g_raw = sbuf(s, "g_raw", [P, 4 * P])
                g_hi = sbuf(s, "g_hi", [P, 4 * P], F32R)
                g_lo = sbuf(s, "g_lo", [P, 4 * P], F32R)
            with ExitStack() as s:
                y_four = sbuf(s, "y_four", [P, 8 * L])
                chan_hi = sbuf(s, "chan_hi", [P, 2, 2 * GW], F32R)
                chan_lo = sbuf(s, "chan_lo", [P, 2, 2 * GW], F32R)
                wf_hi = sbuf(s, "wf_hi", [P, 2, GW], F32R)
                wf_lo = sbuf(s, "wf_lo", [P, 2, GW], F32R)
                wf_raw = sbuf(s, "wf_raw", [P, 2 * GW])
                u_sb = sbuf(s, "u_sb", [P, L])
                eo = sbuf(s, "eo", [P, 2, C])
                eo_hi = sbuf(s, "eo_hi", [P, 2, 2, C], F32R)
                eo_lo = sbuf(s, "eo_lo", [P, 2, 2, C], F32R)
                nyq = sbuf(s, "nyq", [P, 2, 2], F32R)
                nyq_p = sbuf(s, "nyq_p", [P, 10])
                tok_hi = sbuf(s, "tok_hi", [P, 2, 2 * NFREQ], F32R)
                tok_lo = sbuf(s, "tok_lo", [P, 2, 2 * NFREQ], F32R)
                m_hi = sbuf(s, "m_hi", [P, 2, 2 * GW], F32R)
                m_lo = sbuf(s, "m_lo", [P, 2, 2 * GW], F32R)
                p_hi = sbuf(s, "p_hi", [P, 2, 2 * GW], F32R)
                p_lo = sbuf(s, "p_lo", [P, 2, 2 * GW], F32R)
        fin = ExitStack()
        x1 = sbuf(fin, "x1", [P, KT, L])
        acc = sbuf(fin, "acc", [P, KT * L])
        late_par = sbuf(fin, "late_par", [P, NLATE])
        with ExitStack() as s:
            sq1 = sbuf(s, "sq1", [P, 2, L])
            ss1 = sbuf(s, "ss1", [P, L])
        mix.close()
        with ExitStack() as s:
            cg = sbuf(s, "cg", [P, 2, L])
            cv = sbuf(s, "cv", [P, L])
            ss2 = sbuf(s, "ss2", [P, L])
            act_hi = sbuf(s, "act_hi", [P, CH, L], F32R)
            act_lo = sbuf(s, "act_lo", [P, CH, L], F32R)
        fin.close()

        bank = [ctx.enter_context(nc.psum_tensor(f"bank{i}", [P, 512], F32)) for i in range(8)]

        par_in, pos_in, late_in = sem("par_in"), sem("pos_in"), sem("late_in")
        x_in, c_in = [sem(f"x_in{i}") for i in range(4)], sem("c_in")
        raw_in = [sem(f"raw_in{i}") for i in range(RING)]
        hi_done, lo_done = sem("hi_done"), sem("lo_done")
        ada0_used = sem("ada0_used")
        ada_in = [sem(f"ada_in{i}") for i in range(ASLOTS)]
        rows_copied, turned, mod_made = sem("rows_copied"), sem("turned"), sem("mod_made")
        ada_eaten, ada_summed, ada_read = sem("ada_eaten"), sem("ada_summed"), sem("ada_read")
        act_chain, dve_chain = sem("act_chain"), sem("dve_chain")
        csig_done, csil_done, exp_lam, decay_done = sem("csig_done"), sem("csil_done"), sem("exp_lam"), sem("decay_done")
        x_posed, sq_done, sq_added = sem("x_posed"), sem("sq_done"), sem("sq_added")
        totals, std_done, rms_done = sem("totals"), sem("std_done"), sem("rms_done")
        h_pre, h_rounded, h_ready = sem("h_pre"), sem("h_rounded"), sem("h_ready")
        ux_done, ug_done, gates_done = sem("ux_done"), sem("ug_done"), sem("gates_done")
        xc_seed, xc_done, xc_round, xc_split = sem("xc_seed"), sem("xc_done"), sem("xc_round"), sem("xc_split")
        gate_in, gate_hi, gate_lo = sem("gate_in"), sem("gate_hi"), sem("gate_lo")
        gelu_done, gates_read, exp_done, gap_done, root_done, scan_done, head_done = (
            sem(n) for n in ("gelu_done", "gates_read", "exp_done", "gap_done", "root_done", "scan_done", "head_done"))
        tab_in, tab_hi, tab_lo = sem("tab_in"), sem("tab_hi"), sem("tab_lo")
        uf_done, uf_copied, eo_done, eo_rounded, eo_split = (
            sem(n) for n in ("uf_done", "uf_copied", "eo_done", "eo_rounded", "eo_split"))
        m_done, m_rounded, m_split = sem("m_done"), sem("m_rounded"), sem("m_split")
        nyq_done, nyq_read = sem("nyq_done"), sem("nyq_read")
        p_done, p_rounded, p_split = sem("p_done"), sem("p_rounded"), sem("p_split")
        yf_done, yf_read = sem("yf_done"), sem("yf_read")
        yc_rounded, yc_ready = sem("yc_rounded"), sem("yc_ready")
        y_done, y_copied = sem("y_done"), sem("y_copied")
        y_normed, x1_done, x1_squared, x1_summed = (
            sem("y_normed"), (sem("x1_dve"), sem("x1_pool")), sem("x1_squared"), sem("x1_summed"))
        h2_pre, h2_rounded, h2_ready = ((sem(n + "_dve"), sem(n + "_pool")) for n in ("h2_pre", "h2_rounded", "h2_ready"))
        up_half, up_g, up_v, seed_g, seed_v = sem("up_half"), sem("up_g"), sem("up_v"), sem("seed_g"), sem("seed_v")
        conv_g, conv_v, ffn_gelu, ffn_prod = sem("conv_g"), sem("conv_v"), sem("ffn_gelu"), sem("ffn_prod")
        ffn_round, ffn_split = sem("ffn_round"), sem("ffn_split")
        down_done, down_added = sem("down_done"), sem("down_added")
        f_normed, out_ready, stored = sem("f_normed"), (sem("out_dve"), sem("out_pool")), sem("stored")

        def positions(x, tables, k, n):
            piece = x[:, k:k + n, :].rearrange("p k (r c) -> p k r c", c=GRID)
            if k < KT // 2:
                rows = L // GRID
                pos = lcol(tables, "row_pos", rows * k, rows * n).rearrange("p (k r o) -> p k r o", k=n, o=1)
            else:
                pos = lcol(tables, "col_pos", GRID * (k - KT // 2), GRID * n).rearrange("p (k o c) -> p k o c", k=n, o=1)
            return piece, piece, pos.broadcast_to([P, n, L // GRID, GRID])

        block = ctx.enter_context(nc.Block())

        GATE_BANKS = ((3, 5), (6, 1))
        POOL_SUM = [k for k in range(KT) if k % 3 != 2]
        POOL_H2 = [k for k in range(KT) if k % 3 == 2]

        def shared(sems, pool_tiles, k):
            mine = k in pool_tiles
            return sems[mine], sum((j in pool_tiles) == mine for j in range(k + 1))

        R_FOUR = U_HEADS // RING
        R_OUT = R_FOUR + U_FOUR // RING
        R_FFN = R_OUT + U_OUT // RING
        ROUNDS = UNITS // RING
        ADA_ROUNDS = NADA * KT // RING

        @block.sync
        def _(sp):
            def load_unit(rnd, s):
                if isinstance(rnd, int) and rnd == 0:
                    sp.wait_ge(ada0_used, NADA * KT - RING + s + 1)
                else:
                    sp.wait_ge(lo_done, rnd * RING + s - 3)
                sp.dma_start(w_raw[:, s, :], stream[rnd * RING + s]).then_inc(raw_in[s], 16)

            def load_ada(chunk, q):
                if not (isinstance(chunk, int) and chunk == 0 and q < ASLOTS):
                    sp.wait_ge(ada_eaten, chunk * BGU + q - ASLOTS + 1)
                sp.dma_start(ada_raw[:, q % ASLOTS, :], adabg[chunk * BGU + q]).then_inc(ada_in[q % ASLOTS], 16)

            def load_ada0(r):
                for s in range(RING):
                    if not isinstance(r, int) or r > 0:
                        sp.wait_ge(ada0_used, r * RING + s - 3)
                    sp.dma_start(w_raw[:, s, :], ada0[r * RING + s]).then_inc(raw_in[s], 16)

            sp.dma_start(par[:, :], par_d).then_inc(par_in, 16)
            load_ada0(0)
            sp.dma_start(pos0[:, :], late_d[:, 0:NPOS]).then_inc(pos_in, 16)
            for i in range(4):
                sp.dma_start(x0[:, 4 * i:4 * i + 4, :], x_t[:, 4 * i:4 * i + 4, :]).then_inc(x_in[i], 16)
                load_ada0(i + 1)
            sp.dma_start(c0[:, 0:8, :], ctx_t[:, 0:8, :]).then_inc(c_in, 16)
            load_ada0(5)
            sp.dma_start(c0[:, 8:16, :], ctx_t[:, 8:16, :]).then_inc(c_in, 16)
            with sp.Fori(6, ADA_ROUNDS) as r:
                load_ada0(r)
            for s in range(RING):
                load_unit(0, s)

            def head_loads(h):
                if not isinstance(h, int):
                    sp.wait_ge(gate_lo, h)
                sp.dma_start(g_raw[:, :], gates_d[h]).then_inc(gate_in, 16)
                if isinstance(h, int):
                    for q in range(BGU):
                        load_ada(0, q)
                for s in range(RING):
                    load_unit(h + 1, s)
                    load_ada(h + 1, 2 * s)
                    load_ada(h + 1, 2 * s + 1)

            sp.wait_ge(h_ready, KT)
            head_loads(0)
            with sp.Fori(1, HEADS) as h:
                head_loads(h)

            sp.wait_ge(ux_done, HEADS)
            for n in range(4):
                sp.dma_start(y_four[:, ds(n * 2 * NFREQ, 2 * NFREQ)], tabs_d[n]).then_inc(tab_in, 16)
            sp.dma_start(wf_raw[:, :], tabs_d[4, :, 0:2 * GW]).then_inc(tab_in, 16)
            for s in range(RING):
                load_unit(R_FOUR + 1, s)

            def four_loads(g):
                if not isinstance(g, int):
                    sp.wait_ge(tab_lo, g + 5)
                    sp.dma_start(wf_raw[:, :], tabs_d[g + 5, :, 0:2 * GW]).then_inc(tab_in, 16)
                for s in range(RING):
                    load_unit(g + R_FOUR + 2, s)
                    for q in range(4):
                        load_ada(g * 2 + HEADS + 1 + s // 2, 4 * (s % 2) + q)

            with sp.Fori(0, GROUPS - 1) as g:
                four_loads(g)
            four_loads(GROUPS - 1)

            sp.wait_ge(yc_ready, KT)
            def out_loads(i):
                for s in range(RING):
                    load_unit(i + R_OUT + 2, s)
                    for q in range(4):
                        load_ada(i * 2 + HEADS + 2 * GROUPS + 1 + s // 2, 4 * (s % 2) + q)

            sp.dma_start(late_par[:, :], late_d).then_inc(late_in, 16)
            out_loads(0)
            for j in range(4):
                sp.dma_start(x1[:, 4 * j:4 * j + 4, :], x_t[:, 4 * j:4 * j + 4, :]).then_inc(x_in[j], 16)
                out_loads(j + 1)
            out_loads(5)
            for s in range(RING):
                load_unit(R_FFN, s)
                for q in range(2 * s, 2 * s + 2):
                    load_ada(FFN_ADA - 1, q)
            for q in range(ASLOTS):
                load_ada(FFN_ADA, q)
            for s in range(RING):
                load_unit(R_FFN + 1, s)
            for q in range(ASLOTS, BGU):
                load_ada(FFN_ADA, q)
            for q in range(BGU):
                load_ada(FFN_ADA + 1, q)
            with sp.Fori(R_FFN + 2, ROUNDS) as r:
                for s in range(RING):
                    load_unit(r, s)

            for k in range(KT):
                sp.wait_ge(*shared(out_ready, POOL_SUM, k))
                sp.dma_start(out_t[:, k, :], x1[:, k, :]).then_inc(stored, 16)
            sp.wait_ge(stored, 16 * KT)

        @block.gpsimd
        def _(pool):
            def remainders(r, slots=range(RING)):
                for s in slots:
                    pool.wait_ge(hi_done, r * RING + s + 1)
                    nc.gpsimd.tensor_tensor(w_lo[:, s, :], w_raw[:, s, :], w_hi[:, s, :].bitcast(F32),
                                            ALU.subtract).then_inc(lo_done, 1)

            with pool.Fori(0, R_OUT + 5) as r:
                remainders(r)
            pool.wait_ge(late_in, 16)
            for i in range(4):
                pool.wait_ge(x_in[i], 32)
                for half in range(2):
                    nc.gpsimd.tensor_tensor(*positions(x1, late_par, 4 * i + 2 * half, 2), ALU.add).then_inc(x_posed, 1)
                    if i + half < 4:
                        remainders(R_OUT + 5 + i, (2 * half, 2 * half + 1))
            for n, k in enumerate(POOL_SUM):
                pool.wait_ge(y_normed, n + 1)
                nc.gpsimd.tensor_tensor(x1[:, k, :], x1[:, k, :], tile(acc, k), ALU.add).then_inc(x1_done[1], 1)
            remainders(R_FFN, (2, 3))
            pool.wait_ge(rms_done, 4)
            for n in range(len(POOL_H2) + 1):
                if n < len(POOL_H2):
                    k = POOL_H2[n]
                    nc.gpsimd.tensor_tensor(tile(acc, k), x1[:, k, :], ss1[:, :], ALU.mult).then_inc(h2_pre[1], 1)
                if n > 0:
                    k = POOL_H2[n - 1]
                    pool.wait_ge(h2_rounded[1], n)
                    nc.gpsimd.tensor_tensor(h_lo[:, k, :], tile(acc, k), h_hi[:, k, :].bitcast(F32),
                                            ALU.subtract).then_inc(h2_ready[1], 1)
            with pool.Fori(R_FFN + 1, ROUNDS) as r:
                remainders(r)
            for n, k in enumerate(POOL_SUM):
                pool.wait_ge(f_normed, n + 1)
                nc.gpsimd.tensor_tensor(x1[:, k, :], x1[:, k, :], tile(acc, k), ALU.add).then_inc(out_ready[1], 1)

        @block.scalar
        def _(act):
            chain = Chain(act, act_chain)
            sq_n = [0]

            def round_unit(rnd, s):
                act.wait_ge(raw_in[s], rnd * 16 + 16 * (ADA_ROUNDS + 1))
                nc.scalar.activation(w_hi[:, s, :], w_raw[:, s, :], ACT.Copy).then_inc(hi_done, 1)

            def square(dst, src, n):
                if not (isinstance(n, int) and n < 2):
                    act.wait_ge(sq_added, n - 1)
                nc.scalar.activation(dst, src, ACT.Square).then_inc(sq_done, 1)

            def std(n, b, rms):
                act.wait_ge(totals, n + 1)
                nc.scalar.activation(rms, b[:, 0:rms.shape[-1]], ACT.Sqrt, bias=eps[:, :], scale=1.0 / D).then_inc(std_done, 1)

            act.wait_ge(par_in, 16)
            nc.scalar.activation(csil[:, :], pcol("cond"), ACT.Sigmoid).then_inc(csig_done, 1)
            chain.step(nc.scalar.activation(decay[:, 0, :], pcol("lam"), ACT.Abs))
            chain.wait()
            nc.scalar.activation(decay[:, 1, :], decay[:, 0, :], ACT.Exp, scale=-1.0).then_inc(exp_lam, 1)
            def copy_rows(c, half):
                act.wait_ge(ada0_used, 16 * c + 8 * half + 8)
                if c + half > 0:
                    act.wait_ge(turned, 2 * c + half)
                nc.scalar.activation(ada_rows[0:2, :], bank[half][0:2, :], ACT.Copy).then_inc(rows_copied, 1)

            act.wait_ge(decay_done, 1)
            for k in range(KT):
                act.wait_ge(x_posed, k // 4 + 1)
                square(sq0[:, k % 2, :], x0[:, k, :], k)
                if k in (3, 11):
                    copy_rows(0, k // 8)
            act.wait_ge(c_in, 32)
            for k in range(KT):
                square(sq0[:, k % 2, 0:C], c0[:, k, :], KT + k)
            copy_rows(1, 0)
            std(0, bank[6], ss_x[:, :])
            std(1, bank[7], ss_c[:, :])
            for c in range(NADA):
                if c == NADA - 1:
                    round_unit(0, 0)
                if c > 0:
                    copy_rows(c, 1)
                if 0 < c < NADA - 1:
                    copy_rows(c + 1, 0)
                if c == NADA - 1:
                    round_unit(0, 1)
                for k in range(4 * c, 4 * c + 4):
                    act.wait_ge(h_pre, 2 * k + 1)
                    nc.scalar.activation(h_hi[:, k, :], x0[:, k, :], ACT.Identity,
                                         bias=mod_x[:, k:k + 1]).then_inc(h_rounded, 1)
                    act.wait_ge(h_pre, 2 * k + 2)
                    nc.scalar.activation(hc_hi[:, k, :], c0[:, k, :], ACT.Identity,
                                         bias=mod_c[:, k:k + 1]).then_inc(h_rounded, 1)
            round_unit(0, 2)
            round_unit(0, 3)

            def head(h):
                first = isinstance(h, int)
                act.wait_ge(gate_in, h * 16 + 16)
                if not first:
                    act.wait_ge(gates_done, h * 2)
                nc.scalar.activation(g_hi[:, :], g_raw[:, :], ACT.Copy).then_inc(gate_hi, 1)
                act.wait_ge(ux_done, h + 1)
                taps = pcol("lru_conv_w", h * 4 + 2, 1)
                bias = pcol("lru_conv_b", h, 1)
                nc.scalar.activation(xc[:, C:C + L], bank[0][:, :], ACT.Identity, bias=bias, scale=taps).then_inc(xc_seed, 1)
                nc.scalar.activation(xc[:, 0:C], bank[2][:, 0:C], ACT.Identity, bias=bias, scale=taps).then_inc(xc_seed, 1)
                round_unit(h + 1, 0)
                round_unit(h + 1, 1)
                act.wait_ge(xc_done, h + 1)
                nc.scalar.activation(xc_hi[:, :], xc[:, :], ACT.Copy).then_inc(xc_round, 1)
                act.wait_ge(ug_done, h + 1)
                nc.scalar.activation(tile(y_lru, h), bank[1][:, :],
                                     ACT.Gelu_apprx_tanh).then_inc(gelu_done, 1)
                for d in range(2):
                    act.wait_ge(gates_done, h * 2 + d + 1)
                    if not first:
                        act.wait_ge(scan_done, h * 2 + d - 1)
                    br, bi = pcol("gate_b", h * 4 + 2 * d, 1), pcol("gate_b", h * 4 + 2 * d + 1, 1)
                    xb, cb = GATE_BANKS[d]
                    nc.scalar.activation(lru_r[:, d, C:C + L], bank[xb][:, :], ACT.Sigmoid, bias=br)
                    nc.scalar.activation(lru_i[:, d, C:C + L], bank[xb + 1][:, :], ACT.Sigmoid, bias=bi)
                    chain.step(nc.scalar.activation(lru_r[:, d, 0:C], bank[cb][:, 0:C], ACT.Sigmoid, bias=br))
                    nc.scalar.activation(lru_i[:, d, 0:C], bank[cb][:, C:2 * C], ACT.Sigmoid, bias=bi).then_inc(gates_read, 1)
                chain.wait()
                if not first:
                    act.wait_ge(head_done, h)
                for d in range(2):
                    chain.step(nc.scalar.activation(lru_u[:, d, :], lru_r[:, d, :], ACT.Tanh,
                                                    scale=decay[:, 1, ds(h * 2 + d, 1)]))
                for d in range(2):
                    nc.scalar.activation(lru_r[:, d, :], lru_r[:, d, :], ACT.Exp,
                                         scale=decay[:, 2, ds(h * 2 + d, 1)]).then_inc(exp_done, 1)
                round_unit(h + 1, 2)
                round_unit(h + 1, 3)
                for d in range(2):
                    act.wait_ge(gap_done, h * 2 + d + 1)
                    nc.scalar.activation(lru_u[:, d, :], lru_u[:, d, :], ACT.Sqrt).then_inc(root_done, 1)

            head(0)
            with chain.loop(1, HEADS, 4) as h:
                head(h)

            def round_table(n, dst, src):
                act.wait_ge(tab_in, 80 if isinstance(n, int) else n * 16 + 16)
                nc.scalar.activation(dst, src[:, 0:dst.shape[-1]], ACT.Copy).then_inc(tab_hi, 1)

            def fourier_input(g, t):
                n = g * 2 + t
                act.wait_ge(uf_done, n + 1)
                round_unit(g + R_FOUR + 1, 2 * t)
                round_unit(g + R_FOUR + 1, 2 * t + 1)
                if isinstance(g, int) and t == 0:
                    act.wait_ge(head_done, HEADS)
                else:
                    act.wait_ge(eo_split, n)
                nc.scalar.activation(u_sb[:, :], bank[t][:, :], ACT.Copy).then_inc(uf_copied, 1)
                act.wait_ge(eo_done, n + 1)
                if not (isinstance(g, int) and g == 0):
                    act.wait_ge(p_done, g)
                nc.scalar.activation(nyq[:, t, 0:1], u_sb[:, C:C + 1], ACT.Copy)
                nc.scalar.activation(eo_hi[:, t, :, :], eo[:, :, :], ACT.Copy).then_inc(eo_rounded, 1)

            def round_m(g):
                act.wait_ge(m_done, g + 1)
                for t in range(2):
                    nc.scalar.activation(m_hi[:, t, :], bank[6 + t][:, :], ACT.Copy).then_inc(m_rounded, 1)

            def round_p(g):
                act.wait_ge(p_done, g + 1)
                for t in range(2):
                    nc.scalar.activation(p_hi[:, t, :], bank[4 + t][:, :], ACT.Copy).then_inc(p_rounded, 1)

            def round_ycat(n, src):
                nc.scalar.activation(h_hi[:, n, :], src, ACT.Copy).then_inc(yc_rounded, 1)

            wf_all = wf_hi[:, :, :].rearrange("p t d -> p (t d)")
            for n in range(2):
                round_table(n, chan_hi[:, n, :], y_four[:, ds(n * 2 * NFREQ, 2 * NFREQ)])
            round_table(2, wf_all, wf_raw)
            fourier_input(0, 0)
            for n in range(2):
                round_table(n + 3, tok_hi[:, n, :], y_four[:, ds((n + 2) * 2 * NFREQ, 2 * NFREQ)])
            fourier_input(0, 1)
            round_m(0)
            with act.Fori(1, GROUPS) as g:
                act.wait_ge(m_done, g)
                round_table(g + 4, wf_all, wf_raw)
                fourier_input(g, 0)
                round_p(g - 1)
                round_m(g)
                fourier_input(g, 1)
            for n in range(HEADS):
                round_ycat(n, tile(y_lru, n))
                if n == 3:
                    round_p(GROUPS - 1)
            for n in range(8):
                act.wait_ge(yf_read, n // 2 + 1)
                round_ycat(HEADS + n, tile(y_four, n))

            def out_tile(i, t):
                m = i * 2 + t
                act.wait_ge(y_done, m + 1)
                nc.scalar.activation(tile(acc, m), bank[t][:, :], ACT.Copy).then_inc(y_copied, 1)
                square(sq1[:, t, :], bank[t][:, :], m + 2 * KT)

            with act.Fori(0, KT // 2 - 1) as i:
                for t in range(2):
                    out_tile(i, t)
                    round_unit(i + R_OUT + 1, 2 * t)
                    round_unit(i + R_OUT + 1, 2 * t + 1)
            out_tile(KT // 2 - 1, 0)
            round_unit(R_FFN, 0)
            round_unit(R_FFN, 1)
            out_tile(KT // 2 - 1, 1)
            std(2, bank[6], ss1[:, :])
            act.wait_ge(sq_added, 3 * KT)
            for k in range(KT):
                act.wait_ge(*shared(x1_done, POOL_SUM, k))
                if k > 1:
                    act.wait_ge(x1_summed, k - 1)
                nc.scalar.activation(sq1[:, k % 2, :], x1[:, k, :], ACT.Square).then_inc(x1_squared, 1)
                if k in (5, 9):
                    round_unit(R_FFN, 2 + k // 8)
            std(3, bank[5], ss1[:, :])
            act.wait_ge(late_in, 16)
            for k in range(KT):
                shift = mod_x[:, 3 * KT + k:3 * KT + k + 1]
                act.wait_ge(*shared(h2_pre, POOL_H2, k))
                if k in POOL_H2:
                    chain.step(nc.scalar.activation(tile(acc, k), tile(acc, k), ACT.Identity,
                                                    bias=shift, scale=gain_f[:, k:k + 1]))
                    chain.wait()
                    nc.scalar.activation(h_hi[:, k, :], tile(acc, k), ACT.Copy).then_inc(h2_rounded[1], 1)
                else:
                    nc.scalar.activation(h_hi[:, k, :], tile(acc, k), ACT.Identity, bias=shift).then_inc(h2_rounded[0], 1)

            def seed(f, src, dst, tile, done):
                nc.scalar.activation(dst, src, ACT.Identity, bias=lcol(late_par, "ffn_conv_b", tile, 1),
                                     scale=lcol(late_par, "ffn_conv_w", tile * 3 + 1, 1)).then_inc(done, 1)

            def round_act(q):
                nc.scalar.activation(act_hi[:, q, :], cg[:, q % 2, :], ACT.Copy).then_inc(ffn_round, 1)

            def pair(c, p, rnd):
                n = c * CH + p
                if isinstance(c, int) and n == 0:
                    act.wait_ge(up_half, 1)
                    round_unit(rnd, 0)
                    act.wait_ge(up_g, 1)
                else:
                    act.wait_ge(up_g, n + 1)
                    round_unit(rnd, 0)
                round_unit(rnd, 1)
                if not (isinstance(c, int) and p == 0):
                    act.wait_ge(ffn_prod, n)
                    if p > 0 and not isinstance(c, int):
                        act.wait_ge(down_done, c * KT)
                    round_act((p - 1) % CH)
                if not (isinstance(c, int) and p < 2):
                    act.wait_ge(ffn_split, n - 1)
                seed(n, bank[2 * (p % 2)][:, :], cg[:, p % 2, :], n, seed_g)
                act.wait_ge(up_v, n + 1)
                round_unit(rnd, 2)
                round_unit(rnd, 3)
                seed(n, bank[2 * (p % 2) + 1][:, :], cv[:, :], n + FT, seed_v)
                act.wait_ge(conv_g, n + 1)
                nc.scalar.activation(cg[:, p % 2, :], cg[:, p % 2, :], ACT.Gelu_apprx_tanh).then_inc(ffn_gelu, 1)

            for p in range(CH):
                pair(0, p, R_FFN + p + 1)
            with act.Fori(1, NCH) as c:
                r0 = c * 6 + R_FFN - 2
                pair(c, 0, r0 + 1)
                for j in range(4):
                    act.wait_ge(down_done, c * KT + 4 * j + 4 - KT)
                    round_unit(r0 + 2 + j // 2, 2 * (j % 2))
                    round_unit(r0 + 2 + j // 2, 2 * (j % 2) + 1)
                for p in range(1, CH):
                    pair(c, p, r0 + 3 + p)
            act.wait_ge(ffn_prod, FT)
            round_act(CH - 1)
            act.wait_ge(ffn_split, FT)
            act.wait_ge(down_done, (NCH - 1) * KT + 4)
            round_unit(ROUNDS - 1, 0)
            round_unit(ROUNDS - 1, 1)
            act.wait_ge(down_done, (NCH - 1) * KT + 8)
            round_unit(ROUNDS - 1, 2)
            round_unit(ROUNDS - 1, 3)
            for m in range(KT):
                act.wait_ge(down_added, (NCH - 1) * KT + m + 1)
                square(cg[:, m % 2, :], tile(acc, m), m + 3 * KT)
            std(4, bank[0], ss2[:, :])

        @block.tensor
        def _(pe):
            def three(out, w, w_l, v, v_l, start, stop):
                nc.tensor.matmul(out, w, v, start=start, stop=False)
                nc.tensor.matmul(out, w, v_l, start=False, stop=False)
                return nc.tensor.matmul(out, w_l, v, start=False, stop=stop)

            def unit(s, j):
                return w_hi[:, s, P * j:P * j + P], w_lo[:, s, P * j:P * j + P]

            def token_totals(ss, b):
                nc.tensor.matmul(b[:, 0:ss.shape[-1]], ones, ss, start=True, stop=True).then_inc(totals, 1)

            def ada_half(c, half):
                for q in range(8):
                    s = q % RING
                    pe.wait_ge(raw_in[s], c * 64 + 32 * half + 16 * (q // RING) + 16)
                    for i in range(2):
                        k = 2 * q + i
                        mm = nc.tensor.matmul(bank[half][0:2, :], csil[:, 2 * k:2 * k + 2], w_raw[:, s, 512 * i:512 * i + 512],
                                              start=k == 0, stop=k == KT - 1)
                    mm.then_inc(ada0_used, 1)

            def turn(c, half):
                pe.wait_ge(rows_copied, c * 2 + half + 1)
                if half == 0 and not (isinstance(c, int) and c == 0):
                    pe.wait_ge(mod_made, c)
                for j in range(4):
                    mm = nc.tensor.matmul(bank[5][:, 8 * half + 2 * j:8 * half + 2 * j + 2], ada_rows[0:2, P * j:P * j + P],
                                          ident[0:2, 0:2], start=True, stop=True)
                mm.then_inc(turned, 1)

            pe.wait_ge(csil_done, 1)
            ada_half(0, 0)
            ada_half(0, 1)
            turn(0, 0)
            ada_half(1, 0)
            turn(0, 1)
            pe.wait_ge(sq_added, KT)
            token_totals(ss_x[:, :], bank[6])
            ada_half(1, 1)
            pe.wait_ge(sq_added, 2 * KT)
            token_totals(ss_c[:, :], bank[7])
            turn(1, 0)
            with pe.Fori(2, NADA) as c:
                ada_half(c, 0)
                turn(c - 1, 1)
                ada_half(c, 1)
                turn(c, 0)
            turn(NADA - 1, 1)

            def half_job(out, rnd, s, half, ready=None):
                pe.wait_ge(lo_done, rnd * RING + s + half + 1)
                for j in range(8):
                    k = 8 * half + j
                    if ready is not None:
                        pe.wait_ge(*ready(k))
                    w, w_l = unit(s + half, j)
                    mm = three(out, w, w_l, h_hi[:, k, :], h_lo[:, k, :], k == 0, k == KT - 1)
                return mm

            def job(out, rnd, s, ready=None):
                for half in range(2):
                    mm = half_job(out, rnd, s, half, ready)
                return mm

            def sum_ada(n, b):
                pe.wait_ge(ada_eaten, n * BGU + BGU)
                for j in range(2):
                    mm = nc.tensor.matmul(b[:, j:j + 1], ada_acc[:, P * j:P * j + P], ones[:, 0:1], start=True, stop=True)
                mm.then_inc(ada_summed, 1)

            def head(h):
                first = isinstance(h, int)
                for half in range(2):
                    pe.wait_ge(lo_done, h * RING + half + 1)
                    for j in range(8):
                        k = 8 * half + j
                        if first:
                            pe.wait_ge(h_ready, k + 1)
                        w, w_l = unit(half, j)
                        three(bank[0][:, :], w, w_l, h_hi[:, k, :], h_lo[:, k, :], k == 0, k == KT - 1)
                        mm = three(bank[2][:, 0:C], w, w_l, hc_hi[:, k, :], hc_lo[:, k, :], k == 0, k == KT - 1)
                mm.then_inc(ux_done, 1)
                if not first:
                    pe.wait_ge(gates_read, h * 2)
                    sum_ada(h, bank[5])
                mm = job(bank[1][:, :], h, 2)
                mm.then_inc(ug_done, 1)
                if first:
                    sum_ada(h, bank[5])
                pe.wait_ge(xc_split, h + 1)
                pe.wait_ge(gate_lo, h + 1)
                pe.wait_ge(ada_read, h + 1)
                for d in range(2):
                    xb, cb = GATE_BANKS[d]
                    w2 = [(g_hi[:, P * j:P * j + P], g_lo[:, P * j:P * j + P]) for j in (2 * d, 2 * d + 1)]
                    for t, (w, w_l) in enumerate(w2):
                        three(bank[xb + t][:, :], w, w_l, xc_hi[:, C:C + L], xc_lo[:, C:C + L], True, True)
                    if d == 1:
                        pe.wait_ge(gelu_done, h + 1)
                    for t, (w, w_l) in enumerate(w2):
                        mm = three(bank[cb][:, C * t:C * t + C], w, w_l, xc_hi[:, 0:C], xc_lo[:, 0:C], True, True)
                    mm.then_inc(gates_done, 1)

            head(0)
            with pe.Fori(1, HEADS) as h:
                head(h)

            def weights_dft(g):
                pe.wait_ge(tab_lo, g + 5 if not isinstance(g, int) else 3)
                if not isinstance(g, int):
                    pe.wait_ge(m_split, g * 2)
                for t in range(2):
                    for cs in range(2):
                        for j in range(2):
                            at = slice(GW * j + P * t, GW * j + P * t + P)
                            mm = three(bank[6 + t][:, GW * cs:GW * cs + GW], chan_hi[:, cs, at], chan_lo[:, cs, at],
                                       wf_hi[:, j, :], wf_lo[:, j, :], j == 0, j == 1)
                mm.then_inc(m_done, 1)

            def channel_mix(g):
                pe.wait_ge(eo_split, g * 2 + 2)
                pe.wait_ge(m_split, g * 2 + 2)
                for dt in range(2):
                    for t in range(2):
                        for i, m in enumerate((m_hi, m_lo)):
                            mm = nc.tensor.matmul(bank[1][:, 2 * dt:2 * dt + 2], m[:, t, P * dt:P * dt + P], nyq[:, t, :],
                                                  start=(t == 0 and i == 0), stop=(t == 1 and i == 1))
                mm.then_inc(nyq_done, 1)
                for cs in range(2):
                    for nt in range(2):
                        for t in range(2):
                            at = slice(P * nt, P * nt + P)
                            mm = three(bank[4 + cs][:, GW * nt:GW * nt + GW], eo_hi[:, t, cs, at], eo_lo[:, t, cs, at],
                                       m_hi[:, t, GW * cs:GW * cs + GW], m_lo[:, t, GW * cs:GW * cs + GW], t == 0, t == 1)
                mm.then_inc(p_done, 1)

            def token_dft(g, g_next=True):
                pe.wait_ge(p_split, g * 2 + 2)
                pe.wait_ge(m_split, g * 2 + (4 if g_next else 2))
                for dt in range(2):
                    for cs in range(2):
                        out = bank[(2, 6)[dt] + cs]
                        for nt in range(2):
                            at = slice(GW * nt + P * dt, GW * nt + P * dt + P)
                            f = slice(NFREQ * nt, NFREQ * nt + NFREQ)
                            mm = three(out[:, 0:NFREQ], p_hi[:, cs, at], p_lo[:, cs, at],
                                       tok_hi[:, cs, f], tok_lo[:, cs, f], nt == 0, nt == 1)
                mm.then_inc(yf_done, 1)

            def fourier_tile(g, t):
                job(bank[t][:, :], g + R_FOUR, 2 * t).then_inc(uf_done, 1)

            fourier_tile(0, 0)
            pe.wait_ge(gates_read, 2 * HEADS)
            sum_ada(HEADS, bank[3])
            fourier_tile(0, 1)
            weights_dft(0)
            with pe.Fori(1, GROUPS) as g:
                pe.wait_ge(uf_copied, g * 2 - 1)
                fourier_tile(g, 0)
                pe.wait_ge(ada_read, g * 2 + HEADS - 1)
                channel_mix(g - 1)
                weights_dft(g)
                sum_ada(g * 2 + HEADS - 1, bank[3])
                pe.wait_ge(nyq_read, g)
                fourier_tile(g, 1)
                pe.wait_ge(ada_read, g * 2 + HEADS)
                token_dft(g - 1)
                sum_ada(g * 2 + HEADS, bank[4])
            pe.wait_ge(ada_read, HEADS + 2 * GROUPS - 1)
            channel_mix(GROUPS - 1)

            pe.wait_ge(uf_copied, 2 * GROUPS)
            half_job(bank[0][:, :], R_OUT, 0, 0, lambda k: (yc_ready, k + 1))
            pe.wait_ge(yf_read, GROUPS - 1)
            token_dft(GROUPS - 1, False)
            pe.wait_ge(nyq_read, GROUPS)
            half_job(bank[1][:, :], R_OUT, 2, 0)
            half_job(bank[0][:, :], R_OUT, 0, 1, lambda k: (yc_ready, k + 1)).then_inc(y_done, 1)
            half_job(bank[1][:, :], R_OUT, 2, 1).then_inc(y_done, 1)
            AT_OUT = HEADS + 2 * GROUPS - 1
            sum_ada(AT_OUT, bank[3])
            with pe.Fori(1, KT // 2) as i:
                for t in range(2):
                    pe.wait_ge(sq_done, i * 2 + t - 1 + 2 * KT)
                    job(bank[t][:, :], i + R_OUT, 2 * t).then_inc(y_done, 1)
                    pe.wait_ge(ada_read, i * 2 + AT_OUT - 1 + t)
                    sum_ada(i * 2 + AT_OUT - 1 + t, bank[3])
            pe.wait_ge(sq_added, 3 * KT)
            token_totals(ss1[:, :], bank[6])
            for k in range(KT):
                pe.wait_ge(x1_squared, k + 1)
                nc.tensor.matmul(bank[5][:, :], ones, sq1[:, k % 2, :], start=k == 0,
                                 stop=k == KT - 1).then_inc(x1_summed if k < KT - 1 else totals, 1)

            def up_pair(c, p, rnd):
                n = c * CH + p
                if not (isinstance(c, int) and c == 0 and p < 2):
                    pe.wait_ge(conv_v, n - 1)
                b = 2 * (p % 2)
                job(bank[b][:, :], rnd, 0).then_inc(up_g, 1)
                job(bank[b + 1][:, :], rnd, 2).then_inc(up_v, 1)

            def down(c, rnd, at=0):
                if at == 0:
                    pe.wait_ge(ffn_split, c * CH + CH)
                for m in range(at, KT):
                    s, u = m // 2 % RING, m // 2
                    if m % 2 == 0:
                        pe.wait_ge(lo_done, rnd * RING + u + 1)
                    if not (isinstance(c, int) and c == 0 and m < 4):
                        pe.wait_ge(down_added, c * KT + m - 3)
                    for k in range(CH):
                        w, w_l = unit(s, CH * (m % 2) + k)
                        mm = three(bank[4 + m % 4][:, :], w, w_l, act_hi[:, k, :], act_lo[:, k, :], k == 0, k == CH - 1)
                    mm.then_inc(down_done, 1)

            for p in range(CH):
                if p == 0:
                    for half in range(2):
                        pe.wait_ge(lo_done, R_FFN * RING + half + 3)
                        for j in range(8):
                            k = 8 * half + j
                            pe.wait_ge(*shared(h2_ready, POOL_H2, k))
                            for t, done in enumerate((up_g, up_v)):
                                mm = three(bank[t][:, :], *unit(2 * t + half, j), h_hi[:, k, :], h_lo[:, k, :], k == 0, k == KT - 1)
                                if k == KT - 1:
                                    mm.then_inc(done, 1)
                                elif k == 7 and t == 1:
                                    mm.then_inc(up_half, 1)
                else:
                    up_pair(0, p, R_FFN + p)
                if p < 2:
                    sum_ada(FFN_ADA + p, bank[4 + p])
            up_pair(1, 0, R_FFN + CH)
            pe.wait_ge(ada_read, NBG)
            down(0, R_FFN + CH + 1)
            for p in range(1, CH):
                up_pair(1, p, R_FFN + CH + 2 + p)
            with pe.Fori(2, NCH) as c:
                r0 = c * 6 + R_FFN - 2
                up_pair(c, 0, r0)
                down(c - 1, r0 + 1)
                for p in range(1, CH):
                    up_pair(c, p, r0 + 2 + p)
            c, rnd = NCH - 1, ROUNDS - 2
            pe.wait_ge(ffn_split, FT - 1)
            for m in range(4):
                pe.wait_ge(lo_done, rnd * RING + m // 2 + 1)
                pe.wait_ge(down_added, c * KT + m - 3)
                for k in range(CH - 1):
                    three(bank[4 + m][:, :], *unit(m // 2, CH * (m % 2) + k), act_hi[:, k, :], act_lo[:, k, :], k == 0, False)
            pe.wait_ge(ffn_split, FT)
            for m in range(4):
                three(bank[4 + m][:, :], *unit(m // 2, CH * (m % 2) + CH - 1), act_hi[:, CH - 1, :], act_lo[:, CH - 1, :],
                      False, True).then_inc(down_done, 1)
            down(c, rnd, 4)
            pe.wait_ge(sq_added, 4 * KT)
            token_totals(ss2[:, :], bank[0])

        @block.vector
        def _(dve):
            chain = Chain(dve, dve_chain)
            v = nc.vector

            def add_square(ss, sq, n, first=False):
                dve.wait_ge(sq_done, n + 1)
                if first:
                    v.tensor_copy(ss, sq).then_inc(sq_added, 1)
                else:
                    dve.wait_ge(sq_added, n)
                    v.tensor_tensor(ss, ss, sq, ALU.add).then_inc(sq_added, 1)

            def inverse_rms(n, rms):
                dve.wait_ge(std_done, n + 1)
                v.reciprocal(rms, rms).then_inc(rms_done, 1)
                dve.wait_ge(rms_done, n + 1)

            def take_ada(n, b):
                dve.wait_ge(ada_summed, n + 1)
                at = n * 2 + 2 * KT
                v.tensor_tensor(mod_x[:, ds(at, 2)], b[:, 0:2], pcol("b_ada", at, 2), ALU.add).then_inc(ada_read, 1)

            def eat_ada(n, q0, q1):
                for q in range(q0, q1):
                    dve.wait_ge(ada_in[q % ASLOTS], n * (16 * BGU // ASLOTS) + 16 * (q // ASLOTS) + 16)
                    for i in range(2):
                        k = 2 * q + i
                        rows, scale = ada_raw[:, q % ASLOTS, ACOL * i:ACOL * i + ACOL], csil[:, 2 * k:2 * k + 1]
                        if k == 0:
                            ins = v.tensor_scalar(ada_acc[:, :], rows, scale, None, ALU.mult)
                        else:
                            if i == 0:
                                dve.wait_ge(ada_eaten, n * BGU + q)
                            else:
                                chain.wait()
                            ins = v.scalar_tensor_tensor(ada_acc[:, :], rows, scale, ada_acc[:, :], ALU.mult, ALU.add)
                        if i == 0:
                            chain.step(ins)
                        else:
                            ins.then_inc(ada_eaten, 1)

            t1, t2, t3 = (small[:, KT * i:KT * i + KT] for i in range(3))
            dve.wait_ge(csig_done, 1)
            v.tensor_tensor(csil[:, :], csil[:, :], pcol("cond"), ALU.mult).then_inc(csil_done, 1)
            v.memset(eps[:, :], EPS)
            dve.wait_ge(exp_lam, 1)
            chain.step(v.tensor_scalar(t1, decay[:, 1, :], 2.0, None, ALU.add))
            chain.wait()
            chain.step(v.reciprocal(t2, t1))
            chain.wait()
            chain.step(v.tensor_tensor(t1, decay[:, 1, :], t2, ALU.mult))
            chain.wait()
            chain.step(v.tensor_tensor(t2, t1, t1, ALU.mult))
            chain.wait()
            chain.step(v.tensor_scalar(t3, t2, 1.0 / 17, None, ALU.mult))
            for odd in (15, 13, 11, 9, 7, 5, 3):
                chain.wait()
                chain.step(v.scalar_tensor_tensor(t3, t3, 1.0 / odd, t2, ALU.add, ALU.mult))
            chain.wait()
            chain.step(v.scalar_tensor_tensor(t1, t3, 1.0, t1, ALU.add, ALU.mult))
            chain.step(v.tensor_scalar(t2, pcol("lam"), -1.0, 0.0, ALU.mult, ALU.max))
            chain.wait()
            chain.step(v.scalar_tensor_tensor(t3, t1, 2.0, t2, ALU.mult, ALU.add))
            chain.wait()
            chain.step(v.tensor_scalar(decay[:, 1, :], t3, 4.0, None, ALU.mult))
            v.tensor_scalar(decay[:, 2, :], t3, -8.0, None, ALU.mult).then_inc(decay_done, 1)

            dve.wait_ge(pos_in, 16)
            for k in range(KT):
                if k % 4 == 0:
                    dve.wait_ge(x_in[k // 4], 16)
                    v.tensor_tensor(*positions(x0, pos0, k, 4), ALU.add).then_inc(x_posed, 1)
                add_square(ss_x[:, :], sq0[:, k % 2, :], k, first=(k == 0))
            for k in range(KT):
                add_square(ss_c[:, :], sq0[:, k % 2, 0:C], KT + k, first=(k == 0))
            def part(t, c):
                return t[:, 0:2 * KT].rearrange("p (h k) -> p h k", h=2)[:, :, 4 * c:4 * c + 4]

            for c in range(NADA):
                dve.wait_ge(turned, 2 * c + 2)
                both = bank[5][:, 0:16].rearrange("p (h b c) -> p h b c", h=2, c=2)
                chain.step(v.tensor_tensor(part(mod_x, c), both[:, :, :, 0], part(pcol("b_ada"), c), ALU.add))
                v.tensor_tensor(part(mod_c, c), both[:, :, :, 1], part(pcol("b_ada"), c), ALU.add).then_inc(mod_made, 1)
                chain.wait()
                dve.wait_ge(mod_made, c + 1)
                for g, m in ((gain_x, mod_x), (gain_c, mod_c)):
                    chain.step(v.scalar_tensor_tensor(g[:, 4 * c:4 * c + 4], m[:, KT + 4 * c:KT + 4 * c + 4], 1.0,
                                                      pcol("g_mix_pre", 4 * c, 4), ALU.add, ALU.mult))
                chain.wait()
                if c == 0:
                    inverse_rms(0, ss_x[:, :])
                    inverse_rms(1, ss_c[:, :])
                for k in range(4 * c, 4 * c + 5):
                    if k < 4 * c + 4:
                        v.scalar_tensor_tensor(x0[:, k, :], x0[:, k, :], gain_x[:, k:k + 1], ss_x[:, :],
                                               ALU.mult, ALU.mult).then_inc(h_pre, 1)
                        v.scalar_tensor_tensor(c0[:, k, :], c0[:, k, :], gain_c[:, k:k + 1], ss_c[:, :],
                                               ALU.mult, ALU.mult).then_inc(h_pre, 1)
                    if k > 4 * c:
                        j = k - 1
                        dve.wait_ge(h_rounded, 2 * j + 2)
                        v.scalar_tensor_tensor(h_lo[:, j, :], x0[:, j, :], mod_x[:, j:j + 1], h_hi[:, j, :].bitcast(F32),
                                               ALU.add, ALU.subtract)
                        v.scalar_tensor_tensor(hc_lo[:, j, :], c0[:, j, :], mod_c[:, j:j + 1], hc_hi[:, j, :].bitcast(F32),
                                               ALU.add, ALU.subtract).then_inc(h_ready, 1)

            def convolve(h):
                segments = ((bank[0], C, L), (bank[2], 0, C))
                dve.wait_ge(xc_seed, h * 2 + 2)
                for tap, off in ((0, -2), (1, -1), (3, 1)):
                    w = pcol("lru_conv_w", h * 4 + tap, 1)
                    for b, at, n in segments:
                        lo, hi = max(0, -off), min(n, n - off)
                        dst = xc[:, at + lo:at + hi]
                        if tap:
                            chain.wait()
                        ins = v.scalar_tensor_tensor(dst, b[:, lo + off:hi + off], w, dst, ALU.mult, ALU.add)
                        if tap == 3 and at == 0:
                            ins.then_inc(xc_done, 1)
                        else:
                            chain.step(ins)

            def finish_head(h):
                for d in range(2):
                    dve.wait_ge(root_done, h * 2 + d + 1)
                    chain.step(v.tensor_tensor(lru_i[:, d, :], lru_i[:, d, :], lru_u[:, d, :], ALU.mult))
                    chain.wait()
                    if d == 0:
                        ins = v.tensor_tensor_scan(lru_u[:, d, :], lru_r[:, d, :], lru_i[:, d, :], 0.0, ALU.mult, ALU.add)
                    else:
                        a, b, o = (t[:, d, C - 1::-1] for t in (lru_r, lru_i, lru_u))
                        chain.step(v.tensor_tensor_scan(o, a, b, 0.0, ALU.mult, ALU.add))
                        chain.wait()
                        a, b, o = (t[:, d, C + L - 1:C - 1:-1] for t in (lru_r, lru_i, lru_u))
                        ins = v.tensor_tensor_scan(o, a, b, lru_u[:, d, 0:1], ALU.mult, ALU.add)
                    ins.then_inc(scan_done, 1)
                dve.wait_ge(scan_done, h * 2 + 2)
                chain.step(v.tensor_tensor(lru_u[:, 0, C:C + L], lru_u[:, 0, C:C + L], lru_u[:, 1, C:C + L], ALU.add))
                chain.wait()
                dve.wait_ge(gelu_done, h + 1)
                v.tensor_tensor(tile(y_lru, h), tile(y_lru, h), lru_u[:, 0, C:C + L], ALU.mult).then_inc(head_done, 1)

            def head(h):
                first = isinstance(h, int)
                dve.wait_ge(gate_hi, h + 1)
                v.tensor_tensor(g_lo[:, :], g_raw[:, :], g_hi[:, :].bitcast(F32), ALU.subtract).then_inc(gate_lo, 1)
                if first:
                    eat_ada(0, 0, BGU)
                convolve(h)
                dve.wait_ge(xc_round, h + 1)
                v.tensor_tensor(xc_lo[:, :], xc[:, :], xc_hi[:, :].bitcast(F32), ALU.subtract).then_inc(xc_split, 1)
                take_ada(h, bank[5])
                if not first:
                    finish_head(h - 1)
                eat_ada(h + 1, 0, BGU)
                dve.wait_ge(gates_read, h * 2 + 2)
                for d in range(2):
                    chain.step(v.tensor_tensor(lru_i[:, d, :], lru_i[:, d, :], xc[:, :], ALU.mult))
                for d in range(2):
                    dve.wait_ge(exp_done, h * 2 + d + 1)
                    chain.step(v.scalar_tensor_tensor(lru_u[:, d, :], lru_r[:, d, :], 1.0, lru_u[:, d, :], ALU.add, ALU.mult))
                    chain.wait()
                    chain.step(v.tensor_scalar(lru_r[:, d, :], lru_u[:, d, :], -1.0, 1.0, ALU.mult, ALU.add))
                    chain.wait()
                    v.scalar_tensor_tensor(lru_u[:, d, :], lru_r[:, d, :], 1.0, lru_u[:, d, :],
                                           ALU.add, ALU.mult).then_inc(gap_done, 1)

            head(0)
            with chain.loop(1, HEADS, 5 + 4 + 8 + 2 + 4) as h:
                head(h)
            finish_head(HEADS - 1)

            def split_table(n, hi, lo, src):
                dve.wait_ge(tab_hi, n + 1)
                v.tensor_tensor(lo, src[:, 0:hi.shape[-1]], hi.bitcast(F32), ALU.subtract).then_inc(tab_lo, 1)

            def fourier_input(g, t):
                n = g * 2 + t
                dve.wait_ge(uf_copied, n + 1)
                if not (isinstance(g, int) and t == 0):
                    dve.wait_ge(eo_split, n)
                if not isinstance(g, int) and t == 0:
                    chain.wait()
                u, rev = u_sb[:, 1:C], u_sb[:, L - 1:C:-1]
                chain.step(v.tensor_tensor(eo[:, 0, 1:C], u, rev, ALU.add))
                chain.step(v.tensor_tensor(eo[:, 1, 1:C], u, rev, ALU.subtract))
                v.tensor_copy(eo[:, 0, 0:1], u_sb[:, 0:1]).then_inc(eo_done, 1)
                dve.wait_ge(eo_rounded, n + 1)
                chain.step(v.tensor_tensor(nyq[:, t, 1:2], u_sb[:, C:C + 1], nyq[:, t, 0:1].bitcast(F32), ALU.subtract))
                v.tensor_tensor(eo_lo[:, t, :, :], eo[:, :, :], eo_hi[:, t, :, :].bitcast(F32), ALU.subtract).then_inc(eo_split, 1)

            def split_m(g):
                for t in range(2):
                    dve.wait_ge(m_rounded, g * 2 + t + 1)
                    v.tensor_tensor(m_lo[:, t, :], bank[6 + t][:, :], m_hi[:, t, :].bitcast(F32), ALU.subtract).then_inc(m_split, 1)

            def split_p(g):
                for t in range(2):
                    dve.wait_ge(p_rounded, g * 2 + t + 1)
                    v.tensor_tensor(p_lo[:, t, :], bank[4 + t][:, :], p_hi[:, t, :].bitcast(F32), ALU.subtract).then_inc(p_split, 1)

            def read_nyq(g):
                dve.wait_ge(nyq_done, g + 1)
                v.tensor_copy(nyq_p[:, 0:4], bank[1][:, 0:4]).then_inc(nyq_read, 1)
                dve.wait_ge(nyq_read, g + 1)
                two = nyq_p[:, 0:4].rearrange("p (d c) -> p d c", c=2)
                chain.step(v.tensor_tensor(nyq_p[:, 4:6], two[:, :, 0], two[:, :, 1], ALU.add))
                chain.wait()
                bias = pcol("b_fourier", g * 2, 2)
                chain.step(v.tensor_tensor(nyq_p[:, 6:8], bias, nyq_p[:, 4:6], ALU.add))
                chain.step(v.tensor_tensor(nyq_p[:, 8:10], bias, nyq_p[:, 4:6], ALU.subtract))

            def fourier_output(g, g_next=True):
                dve.wait_ge(yf_done, g + 1)
                cosine = eo[:, :, :].rearrange("p t c -> p (t c)")
                dve.wait_ge(eo_split, g * 2 + (4 if g_next else 2))
                for dt in range(2):
                    a, b = bank[(2, 6)[dt]], bank[(3, 7)[dt]]
                    chain.wait()
                    for odd in range(2):
                        chain.step(v.tensor_scalar(cosine[:, odd:NFREQ:2], a[:, odd:NFREQ:2],
                                                   nyq_p[:, 6 + 2 * odd + dt:7 + 2 * odd + dt], None, ALU.add))
                    chain.wait()
                    n = g * 2 + dt
                    v.tensor_tensor(tile(y_four, n, 0, C), cosine[:, 0:C], b[:, 0:C], ALU.subtract)
                    chain.step(v.tensor_copy(tile(y_four, n, C, C + 1), cosine[:, C:C + 1]))
                    last = v.tensor_tensor(tile(y_four, n, C + 1, L), cosine[:, C - 1:0:-1], b[:, C - 1:0:-1], ALU.add)
                    if dt == 0:
                        chain.step(last)
                last.then_inc(yf_read, 1)
                clear_odd()

            def clear_odd():
                chain.wait()
                chain.step(v.memset(eo[:, 1, 0:1], 0.0))

            wf_all = tuple(t[:, :, :].rearrange("p t d -> p (t d)") for t in (wf_hi, wf_lo))
            for n in range(2):
                split_table(n, chan_hi[:, n, :], chan_lo[:, n, :], y_four[:, ds(n * 2 * NFREQ, 2 * NFREQ)])
            split_table(2, *wf_all, wf_raw)
            dve.wait_ge(head_done, HEADS)
            clear_odd()
            fourier_input(0, 0)
            for n in range(2):
                split_table(n + 3, tok_hi[:, n, :], tok_lo[:, n, :], y_four[:, ds((n + 2) * 2 * NFREQ, 2 * NFREQ)])
            take_ada(HEADS, bank[3])
            fourier_input(0, 1)
            split_m(0)
            with chain.loop(1, GROUPS, 16 + 6 + 3 + 8) as g:
                split_table(g + 4, *wf_all, wf_raw)
                eat_ada(g * 2 + HEADS - 1, 0, BGU)
                fourier_input(g, 0)
                read_nyq(g - 1)
                split_p(g - 1)
                split_m(g)
                take_ada(g * 2 + HEADS - 1, bank[3])
                eat_ada(g * 2 + HEADS, 0, BGU)
                fourier_input(g, 1)
                take_ada(g * 2 + HEADS, bank[4])
                fourier_output(g - 1)

            def split_ycat(n, src):
                dve.wait_ge(yc_rounded, n + 1)
                v.tensor_tensor(h_lo[:, n, :], src, h_hi[:, n, :].bitcast(F32), ALU.subtract).then_inc(yc_ready, 1)

            for n in range(4):
                split_ycat(n, tile(y_lru, n))
            read_nyq(GROUPS - 1)
            split_p(GROUPS - 1)
            for n in range(4, HEADS):
                split_ycat(n, tile(y_lru, n))
            fourier_output(GROUPS - 1, False)
            for n in range(8):
                split_ycat(HEADS + n, tile(y_four, n))

            AT_OUT = HEADS + 2 * GROUPS - 1

            def out_tiles(i, ada=2):
                for t in range(2):
                    m = i * 2 + t
                    first = isinstance(i, int) and m == 0
                    if first:
                        eat_ada(AT_OUT, 0, BGU)
                    else:
                        take_ada(m + AT_OUT - 1, bank[3])
                        if t < ada:
                            eat_ada(m + AT_OUT, 0, BGU)
                    add_square(ss1[:, :], sq1[:, t, :], m + 2 * KT, first=first)

            out_tiles(0)
            with chain.loop(1, KT // 2 - 1, 16) as i:
                out_tiles(i)
            dve.wait_ge(late_in, 16)
            chain.step(v.tensor_tensor(gain_y, mod_x[:, 2 * KT:3 * KT], pcol("g_mix_post"), ALU.mult))
            out_tiles(KT // 2 - 1, 1)
            dve.wait_ge(ada_read, FFN_ADA)
            chain.step(v.scalar_tensor_tensor(gain_f, mod_x[:, 4 * KT:5 * KT], 1.0, pcol("g_ffn_pre"), ALU.add, ALU.mult))
            inverse_rms(2, ss1[:, :])
            dve.wait_ge(x_posed, 12)
            for k in range(KT):
                ins = v.scalar_tensor_tensor(tile(acc, k), tile(acc, k), gain_y[:, k:k + 1], ss1[:, :], ALU.mult, ALU.mult)
                if k in POOL_SUM:
                    ins.then_inc(y_normed, 1)
                else:
                    chain.step(ins)
                    chain.wait()
                    v.tensor_tensor(x1[:, k, :], x1[:, k, :], tile(acc, k), ALU.add).then_inc(x1_done[0], 1)
            dve.wait_ge(y_normed, len(POOL_SUM))
            inverse_rms(3, ss1[:, :])
            mine = [k for k in range(KT) if k not in POOL_H2]
            for n in range(len(mine) + 1):
                if n < len(mine):
                    k = mine[n]
                    v.scalar_tensor_tensor(tile(acc, k), x1[:, k, :], gain_f[:, k:k + 1], ss1[:, :],
                                           ALU.mult, ALU.mult).then_inc(h2_pre[0], 1)
                if n > 0:
                    k = mine[n - 1]
                    dve.wait_ge(h2_rounded[0], n)
                    v.scalar_tensor_tensor(h_lo[:, k, :], tile(acc, k), mod_x[:, 3 * KT + k:3 * KT + k + 1],
                                           h_hi[:, k, :].bitcast(F32), ALU.add, ALU.subtract).then_inc(h2_ready[0], 1)
            eat_ada(FFN_ADA, 0, BGU)

            def convolve_ffn(b, dst, tile_no, done):
                chain.step(v.scalar_tensor_tensor(dst[:, 1:L], b[:, 0:L - 1], lcol(late_par, "ffn_conv_w", tile_no * 3, 1), dst[:, 1:L],
                                                  ALU.mult, ALU.add))
                chain.wait()
                v.scalar_tensor_tensor(dst[:, 0:L - 1], b[:, 1:L], lcol(late_par, "ffn_conv_w", tile_no * 3 + 2, 1), dst[:, 0:L - 1],
                                       ALU.mult, ALU.add).then_inc(done, 1)

            def split_act(n, q):
                dve.wait_ge(ffn_round, n + 1)
                v.tensor_tensor(act_lo[:, q, :], cg[:, q % 2, :], act_hi[:, q, :].bitcast(F32), ALU.subtract).then_inc(ffn_split, 1)

            def pair(c, p):
                n = c * CH + p
                if not (isinstance(c, int) and n == 0):
                    split_act(n - 1, (p - 1) % CH)
                dve.wait_ge(seed_g, n + 1)
                convolve_ffn(bank[2 * (p % 2)], cg[:, p % 2, :], n, conv_g)
                dve.wait_ge(seed_v, n + 1)
                convolve_ffn(bank[2 * (p % 2) + 1], cv[:, :], n + FT, conv_v)
                dve.wait_ge(conv_v, n + 1)
                dve.wait_ge(ffn_gelu, n + 1)
                v.tensor_tensor(cg[:, p % 2, :], cg[:, p % 2, :], cv[:, :], ALU.mult).then_inc(ffn_prod, 1)

            def add_down(c, m):
                dve.wait_ge(down_done, c * KT + m + 1)
                if isinstance(c, int) and c == 0:
                    v.tensor_copy(tile(acc, m), bank[4 + m % 4][:, :]).then_inc(down_added, 1)
                else:
                    v.tensor_tensor(tile(acc, m), tile(acc, m), bank[4 + m % 4][:, :], ALU.add).then_inc(down_added, 1)

            def chunk(c):
                pair(c, 0)
                for m in range(KT):
                    add_down(c - 1, m)
                for p in range(1, CH):
                    pair(c, p)

            for p in range(CH):
                pair(0, p)
                if p < 2:
                    take_ada(FFN_ADA + p, bank[4 + p])
                if p == 0:
                    eat_ada(FFN_ADA + 1, 0, BGU)
                    dve.wait_ge(ada_eaten, NBG * BGU)
                elif p == 1:
                    dve.wait_ge(ada_read, NBG)
                    chain.step(v.tensor_tensor(gain_d, mod_x[:, 5 * KT:6 * KT], pcol("g_ffn_post"), ALU.mult))
            chunk(1)
            with chain.loop(2, NCH, 2 * CH) as c:
                chunk(c)
            split_act(FT - 1, CH - 1)
            for m in range(KT):
                add_down(NCH - 1, m)
                for j in range(2 * m - KT, 2 * m - KT + 2):
                    if j >= 0:
                        add_square(ss2[:, :], cg[:, j % 2, :], j + 3 * KT, first=(j == 0))
            inverse_rms(4, ss2[:, :])
            for k in range(KT):
                ins = v.scalar_tensor_tensor(tile(acc, k), tile(acc, k), gain_d[:, k:k + 1], ss2[:, :], ALU.mult, ALU.mult)
                if k in POOL_SUM:
                    ins.then_inc(f_normed, 1)
                else:
                    chain.step(ins)
                    chain.wait()
                    v.tensor_tensor(x1[:, k, :], x1[:, k, :], tile(acc, k), ALU.add).then_inc(out_ready[0], 1)


def dft_tables():
    j, c = np.arange(GW)[:, None], np.arange(GW)[None, :]
    turn = 2 * np.pi * ((j * c) % GW) / GW
    scale = 1 / np.sqrt(L * GW)
    n, k = np.arange(L // 2)[:, None], np.arange(NFREQ)[None, :]
    turn_tok = 2 * np.pi * ((n * k) % L) / L
    sines = np.sin(turn_tok)
    sines[(2 * n * k) % L == 0] = 0.0
    out = np.zeros((4, P, 2 * NFREQ), np.float32)
    for t, table in enumerate((np.cos(turn) * scale, np.sin(turn) * scale, np.cos(turn_tok), sines)):
        width = 2 * table.shape[1]
        out[t, :, :width] = table.reshape(2, P, -1).transpose(1, 0, 2).reshape(P, width)
    return out


def position_tables():
    quarter = D // 4
    freqs = np.float32(10000.0) ** (-np.arange(quarter, dtype=np.float32) / np.float32(quarter))
    out = []
    for n in (L // GRID, GRID):
        angle = (np.arange(n, dtype=np.float32)[:, None] * freqs[None, :]).astype(np.float64)
        enc = np.concatenate([np.sin(angle), np.cos(angle)], axis=-1).astype(np.float32)
        out.append(enc.T)
    return out


def columns(a):
    a = a.reshape(-1, P, *a.shape[1:])
    return np.moveaxis(a, 1, 0).reshape(P, -1)


def kernel(**inputs):
    import concourse.bacc as bacc
    from concourse.bass_utils import run_bass_kernel_spmd

    a = {k: np.asarray(val) for k, val in inputs.items()}
    w = {k: a[k][0] for k in a if k not in ("x", "c", "ctx", "c_ctx")}

    def feature_tiles(x):
        return np.ascontiguousarray(x.T.reshape(KT, P, -1).transpose(1, 0, 2))

    def units16(m):
        return m.reshape(2, 8, P, -1, P).transpose(3, 0, 2, 1, 4).reshape(-1, 2, P, UNIT)

    w_in = units16(w["w_in"])
    w_out = units16(np.concatenate([w["w_out"][D // 2:], w["w_out"][:D // 2]]))
    w_up = units16(w["w_up"])
    w_down = w["w_down"].reshape(NCH, CH, P, 8, 2, P).transpose(0, 3, 2, 4, 1, 5).reshape(NCH, 8, P, UNIT)
    parts = []
    for h in range(HEADS):
        parts += [w_in[8 + h], w_in[16 + h]]
    parts += [w_in[m] for m in range(8)] + [w_out[m] for m in range(KT)]
    for c in range(NCH):
        for p in range(CH):
            parts += [w_up[c * CH + p], w_up[FT + c * CH + p]]
            if p == 0 and c > 0:
                parts.append(w_down[c - 1])
    parts.append(w_down[NCH - 1])
    stream = np.concatenate(parts)
    assert stream.shape == (UNITS, P, UNIT)

    ada = w["w_ada"]
    ada0 = ada[:, :1024 * NADA].reshape(8, 2, P, 2, NADA, 512).transpose(4, 3, 0, 2, 1, 5).reshape(-1, P, 1024)
    adabg = ada[:, 1024 * NADA:].reshape(BGU, 2, P, NBG, ACOL).transpose(3, 0, 2, 1, 4).reshape(-1, P, 2 * ACOL)
    gates = np.stack([w["w_rec_gate"][0], w["w_in_gate"][0], w["w_rec_gate"][1], w["w_in_gate"][1]], axis=2)
    gates = gates.reshape(HEADS, P, 4 * P)
    wf = w["w_fourier"].reshape(GROUPS, 2, P, GW).transpose(0, 2, 1, 3).reshape(GROUPS, P, 2 * GW)
    tabs = np.concatenate([dft_tables(), np.pad(wf, ((0, 0), (0, 0), (0, 2 * NFREQ - 2 * GW)))])
    row_pos, col_pos = position_tables()
    per_head = {
        "lam": w["lru_lambda"].T,
        "lru_conv_w": w["conv_lru_w"].T,
        "gate_b": np.stack([w["b_rec_gate"][0], w["b_in_gate"][0], w["b_rec_gate"][1], w["b_in_gate"][1]], axis=1),
        "ffn_conv_w": w["conv_ffn_w"].T,
        "cond": np.stack([a["c"][0], a["c_ctx"]], axis=1),
        "row_pos": row_pos, "col_pos": col_pos,
        "ones": np.ones((P, P), np.float32), "ident": np.eye(P, dtype=np.float32),
        "lru_conv_b": w["conv_lru_b"], "ffn_conv_b": w["conv_ffn_b"],
    }
    par = np.concatenate([columns(per_head.get(n, w.get(n))) for n in PAR], axis=1)
    late = np.concatenate([columns(per_head[n]) for n in LATE], axis=1)
    assert par.shape == (P, NPAR) and late.shape == (P, NLATE)

    arrays = {"x_t": feature_tiles(a["x"][0]), "ctx_t": feature_tiles(a["ctx"][0]), "par": par, "late": late, "stream": stream, "ada0": ada0,
              "adabg": adabg, "gates": gates, "tabs": tabs}
    nc = bacc.Bacc("TRN2", target_bir_lowering=False, num_devices=1)
    arrays = {f"in_{n}": np.ascontiguousarray(val) for n, val in arrays.items()}
    args = [nc.dram_tensor(n, val.shape, F32, kind="ExternalInput").ap() for n, val in arrays.items()]
    out = nc.dram_tensor("out_t", (P, KT, L), F32, kind="ExternalOutput").ap()
    build(nc, *args, out)
    r = run_bass_kernel_spmd(nc, [arrays], core_ids=[0])
    got = np.asarray(r.results[0]["out_t"])
    return np.ascontiguousarray(got.transpose(1, 0, 2).reshape(D, L).T)[None]
```
